# Optimizing a Trainium2 kernel written in Bass

```python
import math
import jax, jax.numpy as jnp
from jax import lax
import numpy as np

D_MODEL = 1024
BATCH = 1
SEQ = 256
DEPTH = 2
DEC_BATCH = 8
DEC_SEQ = 16
PAST_LEN = 128

CHUNK = 64
N_META = 16
MIX_WIDTH = D_MODEL
ATTN_WIDTH = MIX_WIDTH // 2
POOL_WIDTH = MIX_WIDTH - ATTN_WIDTH
HEAD_DIM = 64
N_HEADS = ATTN_WIDTH // (2 * HEAD_DIM)
POOL_WINDOWS = (2, 4, 8, 16)
N_POOL_GROUPS = len(POOL_WINDOWS)
POOL_GROUP_WIDTH = POOL_WIDTH // N_POOL_GROUPS
POOL_STATE = max(POOL_WINDOWS) - 1
IN_COLS = 3 * ATTN_WIDTH + POOL_WIDTH
N_EXPERTS = 16
N_EXPERT_GROUPS = 4
EXPERTS_PER_GROUP = N_EXPERTS // N_EXPERT_GROUPS
TOP_K = 2
D_EXPERT = D_MODEL // 2
Q_BLOCK = 128
ALPHA = (2 * DEPTH) ** 0.25
BETA = (8 * DEPTH) ** -0.25
LN_EPS = 1e-5

kernel_name = 'hybrid_stream_diffattn_pool_grouped_moe'

def layer_norm(x, g, b):
    xf = x.astype(jnp.float32)
    mu = jnp.mean(xf, axis=-1, keepdims=True)
    var = jnp.mean(jnp.square(xf - mu), axis=-1, keepdims=True)
    y = (xf - mu) * lax.rsqrt(var + LN_EPS) * g.astype(jnp.float32) + b.astype(jnp.float32)
    return y.astype(x.dtype)

def alibi_slopes():
    return 2.0 ** (-8.0 * jnp.arange(1, N_HEADS + 1, dtype=jnp.float32) / N_HEADS)

def lambda_init(layer):
    return 0.8 - 0.6 * math.exp(-0.3 * layer)

def diff_lambda(lam_qk, lam_init):
    lq = lam_qk.astype(jnp.float32)
    return jnp.exp(jnp.sum(lq[0] * lq[1])) - jnp.exp(jnp.sum(lq[2] * lq[3])) + lam_init

def diff_attention(q, k, v, q_pos, k_pos, q_chunk, k_chunk, lam, subln_w, lam_init):
    q1, q2 = q[..., :HEAD_DIM].astype(jnp.float32), q[..., HEAD_DIM:].astype(jnp.float32)
    k1, k2 = k[..., :HEAD_DIM].astype(jnp.float32), k[..., HEAD_DIM:].astype(jnp.float32)
    dist = jnp.abs(q_pos[:, None] - k_pos[None, :]).astype(jnp.float32)
    bias = -alibi_slopes()[:, None, None] * dist[None]
    visible = k_chunk[None, :] <= q_chunk[:, None]
    scale = HEAD_DIM ** -0.5

    def softmax_map(qa, ka):
        s = jnp.einsum('bqhd,bkhd->bhqk', qa, ka) * scale + bias
        return jax.nn.softmax(jnp.where(visible, s, -jnp.inf), axis=-1)

    weights = softmax_map(q1, k1) - lam * softmax_map(q2, k2)
    o = jnp.einsum('bhqk,bkhe->bqhe', weights, v.astype(jnp.float32))
    o = o * lax.rsqrt(jnp.mean(jnp.square(o), axis=-1, keepdims=True) + LN_EPS)
    o = o * subln_w.astype(jnp.float32) * (1.0 - lam_init)
    return o.astype(q.dtype)

def prompt_attention(q, k, v, lam, subln_w, lam_init):
    B, L = q.shape[0], q.shape[1]
    pos = jnp.arange(L, dtype=jnp.int32)
    chunk = jnp.where(pos < N_META, -1, (pos - N_META) // CHUNK)
    meta_out = diff_attention(q[:, :N_META], k[:, :N_META], v[:, :N_META], pos[:N_META], pos[:N_META],
                              chunk[:N_META], chunk[:N_META], lam, subln_w, lam_init)
    n_blk = (L - N_META) // Q_BLOCK
    qb = q[:, N_META:].reshape(B, n_blk, Q_BLOCK, N_HEADS, 2 * HEAD_DIM).transpose(1, 0, 2, 3, 4)
    pb = pos[N_META:].reshape(n_blk, Q_BLOCK)
    cb = chunk[N_META:].reshape(n_blk, Q_BLOCK)

    def one_block(args):
        qi, pi, ci = args
        return diff_attention(qi, k, v, pi, pos, ci, chunk, lam, subln_w, lam_init)

    out = lax.map(one_block, (qb, pb, cb))
    real_out = out.transpose(1, 0, 2, 3, 4).reshape(B, L - N_META, N_HEADS, 2 * HEAD_DIM)
    return jnp.concatenate([meta_out, real_out], axis=1)

def pool_mixer(u_ext, pos0, n_out, w_pool_l, scale_l):
    B, T, _ = u_ext.shape
    uf = u_ext.astype(jnp.float32)
    cs = jnp.pad(jnp.cumsum(uf, axis=1), ((0, 0), (1, 0), (0, 0)))
    pos = pos0 + jnp.arange(T, dtype=jnp.int32)
    diffs = []
    for g, w in enumerate(POOL_WINDOWS):
        lo, hi = g * POOL_GROUP_WIDTH, (g + 1) * POOL_GROUP_WIDTH
        c = cs[..., lo:hi]
        lagged = jnp.pad(c, ((0, 0), (w, 0), (0, 0)))[:, 1:T + 1]
        window_sum = c[:, 1:] - lagged
        count = jnp.minimum(pos + 1, w).astype(jnp.float32)[:, None]
        diffs.append(window_sum / count - uf[..., lo:hi])
    d = jnp.stack(diffs, axis=2)[:, T - n_out:]
    y = jnp.einsum('btgc,gce->btge', d, w_pool_l.astype(jnp.float32))
    y = y * scale_l.astype(jnp.float32).reshape(N_POOL_GROUPS, POOL_GROUP_WIDTH)
    return y.reshape(B, n_out, POOL_WIDTH).astype(u_ext.dtype)

def split_projection(h, w_in_l):
    B, T, _ = h.shape
    proj = jnp.einsum('btd,de->bte', h, w_in_l)
    q = proj[..., :ATTN_WIDTH].reshape(B, T, N_HEADS, 2 * HEAD_DIM)
    k = proj[..., ATTN_WIDTH:2 * ATTN_WIDTH].reshape(B, T, N_HEADS, 2 * HEAD_DIM)
    v = proj[..., 2 * ATTN_WIDTH:3 * ATTN_WIDTH].reshape(B, T, N_HEADS, 2 * HEAD_DIM)
    u = proj[..., 3 * ATTN_WIDTH:]
    return q, k, v, u

def merge_and_residual(h, attn_out, pool_out, w_out_l, g, b):
    B, T, _ = h.shape
    mix = jnp.concatenate([attn_out.reshape(B, T, ATTN_WIDTH), pool_out], axis=-1)
    return layer_norm(ALPHA * h + jnp.einsum('bte,ed->btd', mix, w_out_l), g, b)

def moe_ffn(h, router_w, router_b, w_gate_l, w_up_l, w_down_l):
    B, T, D = h.shape
    xf = h.reshape(B * T, D)
    probs = jax.nn.softmax(jnp.einsum('nd,de->ne', xf.astype(jnp.float32), router_w.astype(jnp.float32)), axis=-1)
    sel = (probs + router_b.astype(jnp.float32)).reshape(-1, N_EXPERT_GROUPS, EXPERTS_PER_GROUP)
    group_score = jnp.sum(lax.top_k(sel, TOP_K)[0], axis=-1)
    g_idx = jnp.argmax(group_score, axis=-1)
    in_group = jnp.take_along_axis(sel, g_idx[:, None, None], axis=1)[:, 0]
    _, e_local = lax.top_k(in_group, TOP_K)
    e_idx = g_idx[:, None] * EXPERTS_PER_GROUP + e_local
    gate = jnp.take_along_axis(probs, e_idx, axis=1)
    gate = gate / jnp.sum(gate, axis=-1, keepdims=True)
    combine = jnp.einsum('nk,nke->ne', gate, jax.nn.one_hot(e_idx, N_EXPERTS, dtype=jnp.float32))
    y = jnp.zeros((B * T, D), jnp.float32)
    for e in range(N_EXPERTS):
        hid = jax.nn.silu(xf @ w_gate_l[e]) * (xf @ w_up_l[e])
        y = y + combine[:, e:e + 1] * (hid @ w_down_l[e]).astype(jnp.float32)
    return y.reshape(B, T, D).astype(h.dtype)

def setup_inputs(seed: int = 0) -> dict:
    key = jax.random.key(seed)
    ks = jax.random.split(key, 24)
    f32 = jnp.float32

    def nrm(k, shape, scale):
        return jax.random.normal(k, shape, f32) * scale

    v_col_scale = jnp.ones((IN_COLS,), f32).at[2 * ATTN_WIDTH:3 * ATTN_WIDTH].set(BETA)
    return {
        'x_prompt': nrm(ks[0], (BATCH, SEQ, D_MODEL), 1.0),
        'x_sample': nrm(ks[1], (DEC_BATCH, DEC_SEQ, D_MODEL), 1.0),
        'cache_k': nrm(ks[2], (DEPTH, DEC_BATCH, PAST_LEN, N_HEADS, 2 * HEAD_DIM), 1.0),
        'cache_v': nrm(ks[3], (DEPTH, DEC_BATCH, PAST_LEN, N_HEADS, 2 * HEAD_DIM), BETA),
        'state_pool': nrm(ks[4], (DEPTH, DEC_BATCH, POOL_STATE, POOL_WIDTH), 1.0),
        'meta_tokens': nrm(ks[5], (N_META, D_MODEL), 1.0),
        'ln_in_g': 1.0 + nrm(ks[6], (D_MODEL,), 0.05),
        'ln_in_b': nrm(ks[7], (D_MODEL,), 0.02),
        'w_in': nrm(ks[8], (DEPTH, D_MODEL, IN_COLS), D_MODEL ** -0.5) * v_col_scale,
        'lambda_qk': nrm(ks[9], (DEPTH, 4, HEAD_DIM), 0.1),
        'subln_w': 1.0 + nrm(ks[10], (DEPTH, 2 * HEAD_DIM), 0.05),
        'w_pool': nrm(ks[11], (DEPTH, N_POOL_GROUPS, POOL_GROUP_WIDTH, POOL_GROUP_WIDTH), POOL_GROUP_WIDTH ** -0.5),
        'pool_scale': 1.0 + nrm(ks[12], (DEPTH, POOL_WIDTH), 0.1),
        'w_out': nrm(ks[13], (DEPTH, MIX_WIDTH, D_MODEL), MIX_WIDTH ** -0.5 * BETA),
        'ln1_g': 1.0 + nrm(ks[14], (DEPTH, D_MODEL), 0.05),
        'ln1_b': nrm(ks[15], (DEPTH, D_MODEL), 0.02),
        'router_w': nrm(ks[16], (D_MODEL, N_EXPERTS), D_MODEL ** -0.5),
        'router_b': nrm(ks[17], (N_EXPERTS,), 0.01),
        'w_gate': nrm(ks[18], (DEPTH, N_EXPERTS, D_MODEL, D_EXPERT), D_MODEL ** -0.5),
        'w_up': nrm(ks[19], (DEPTH, N_EXPERTS, D_MODEL, D_EXPERT), D_MODEL ** -0.5),
        'w_down': nrm(ks[20], (DEPTH, N_EXPERTS, D_EXPERT, D_MODEL), D_EXPERT ** -0.5 * BETA),
        'ln2_g': 1.0 + nrm(ks[21], (DEPTH, D_MODEL), 0.05),
        'ln2_b': nrm(ks[22], (DEPTH, D_MODEL), 0.02),
    }

def reference(x_prompt, x_sample, cache_k, cache_v, state_pool, meta_tokens, ln_in_g, ln_in_b, w_in, lambda_qk,
              subln_w, w_pool, pool_scale, w_out, ln1_g, ln1_b, router_w, router_b, w_gate, w_up, w_down,
              ln2_g, ln2_b):
    B, S, D = x_prompt.shape
    L = N_META + S
    meta = jnp.broadcast_to(meta_tokens[None].astype(x_prompt.dtype), (B, N_META, D))
    h = layer_norm(jnp.concatenate([meta, x_prompt], axis=1), ln_in_g, ln_in_b)
    k_rows, v_rows, pool_rows = [], [], []
    for l in range(DEPTH):
        lam_init = lambda_init(l)
        lam = diff_lambda(lambda_qk[l], lam_init)
        q, k, v, u = split_projection(h, w_in[l])
        a = prompt_attention(q, k, v, lam, subln_w[l], lam_init)
        p = pool_mixer(u, 0, L, w_pool[l], pool_scale[l])
        h = merge_and_residual(h, a, p, w_out[l], ln1_g[l], ln1_b[l])
        h = layer_norm(ALPHA * h + moe_ffn(h, router_w, router_b, w_gate[l], w_up[l], w_down[l]), ln2_g[l], ln2_b[l])
        k_rows.append(k)
        v_rows.append(v)
        pool_rows.append(u[:, L - POOL_STATE:])
    y_prompt = h[:, N_META:]

    T = x_sample.shape[1]
    P = cache_k.shape[2]
    k_pos = jnp.arange(P + T, dtype=jnp.int32)
    q_pos = k_pos[P:]
    hs = layer_norm(x_sample, ln_in_g, ln_in_b)
    ks_rows, vs_rows, pools_rows = [], [], []
    for l in range(DEPTH):
        lam_init = lambda_init(l)
        lam = diff_lambda(lambda_qk[l], lam_init)
        q, k, v, u = split_projection(hs, w_in[l])
        k_all = jnp.concatenate([cache_k[l].astype(k.dtype), k], axis=1)
        v_all = jnp.concatenate([cache_v[l].astype(v.dtype), v], axis=1)
        a = diff_attention(q, k_all, v_all, q_pos, k_pos, q_pos // CHUNK, k_pos // CHUNK, lam, subln_w[l], lam_init)
        u_ext = jnp.concatenate([state_pool[l].astype(u.dtype), u], axis=1)
        p = pool_mixer(u_ext, P - POOL_STATE, T, w_pool[l], pool_scale[l])
        hs = merge_and_residual(hs, a, p, w_out[l], ln1_g[l], ln1_b[l])
        hs = layer_norm(ALPHA * hs + moe_ffn(hs, router_w, router_b, w_gate[l], w_up[l], w_down[l]), ln2_g[l], ln2_b[l])
        ks_rows.append(k)
        vs_rows.append(v)
        pools_rows.append(u_ext[:, T:])
    y_sample = hs

    new_k_prompt = jnp.stack(k_rows, axis=0)
    new_v_prompt = jnp.stack(v_rows, axis=0)
    new_pool_prompt = jnp.stack(pool_rows, axis=0)
    new_k_sample = jnp.stack(ks_rows, axis=0)
    new_v_sample = jnp.stack(vs_rows, axis=0)
    new_pool_sample = jnp.stack(pools_rows, axis=0)
    return (y_prompt, y_sample, new_k_prompt, new_v_prompt, new_pool_prompt, new_k_sample, new_v_sample, new_pool_sample)


_drawn_inputs = setup_inputs


def setup_inputs(seed=0):
    import zlib

    import numpy as np

    out = dict(_drawn_inputs(seed))
    spreads = {}
    factors = {}
    for name, (base, spread) in spreads.items():
        noise = np.random.default_rng([zlib.crc32(name.encode()), seed]).standard_normal(out[name].shape)
        drawn = base * np.exp(spread * noise) if base else spread * noise
        out[name] = __import__('jax').numpy.asarray(drawn.astype(out[name].dtype))
    for name, factor in factors.items():
        out[name] = (out[name] * factor).astype(out[name].dtype)
    return out
```

```python
from contextlib import ExitStack

import numpy as np
import concourse.bass as bass
from concourse import mybir

F32 = mybir.dt.float32
I32 = mybir.dt.int32
U32 = mybir.dt.uint32
ALU = mybir.AluOpType
ACT = mybir.ActivationFunctionType
X = mybir.AxisListType.X

DEPTH, D, NMETA, SEQ, DB, DS, PAST = 2, 1024, 16, 256, 8, 16, 128
P = 128
KT = D // P
HEADS, HD = 4, 64
AW = HEADS * 2 * HD
NTOK = NMETA + SEQ + DB * DS
TC = [16, 144, 272, 0]
TN = [128, 128, 128, 16]
DEC = TC[2]
NE, NG, EPG = 16, 4, 4
DE = 512
ALPHA = float((2 * DEPTH) ** 0.25)
EPS = 1e-5
STATE = 15
WINDOWS = (2, 4, 8, 16)
SLOTS = 6
CH = 4096
SCALE = HD ** -0.5
NEG = -1e30
FAR = 4096.0
PAIRS = NE // 2
LAM_INIT = [0.8 - 0.6 * float(np.exp(-0.3 * l)) for l in range(DEPTH)]
SLOPES = [2.0 ** (-8.0 * h / HEADS) for h in range(1, HEADS + 1)]

C_ID, C_TRI, C_ONE, C_D1, C_D0, C_DD, C_DM = 0, 128, 256, 384, 656, 800, 1056
C_IOTA, C_PG, C_PE, C_ROW, C_POOL, C_VALID, C_HALF, C_END = 1184, 1312, 1316, 1332, 1340, 1404, 1408, 1410


def const_table():
    c = np.zeros((P, C_END), np.float32)
    i = np.arange(P)
    c[:, C_ID:C_ID + P] = np.eye(P)
    c[:, C_TRI:C_TRI + P] = i[:, None] < i[None, :]
    c[:, C_ONE:C_ONE + P] = 1.0
    kpos = np.arange(NMETA + SEQ)
    kch = np.where(kpos < NMETA, -1, (kpos - NMETA) // 64)

    def dist(qp, kp, seen):
        return np.where(seen, -np.abs(qp[:, None] - kp[None, :]), NEG).astype(np.float32)

    for col, first, n in ((C_D1, 128, 272), (C_D0, 0, 144)):
        qpos = NMETA + first + i
        c[:, col:col + n] = dist(qpos, kpos[:n], kch[None, :n] <= ((qpos - NMETA) // 64)[:, None])
    b, t = i // DS, i % DS
    c[:, C_DD:C_DD + P] = dist(PAST + t, np.arange(P), np.ones((P, P), bool))
    c[:, C_DD + P:C_DD + 2 * P] = dist(PAST + t, PAST + t, b[:, None] == b[None, :])
    m = np.arange(NMETA)
    for h in range(HEADS):
        for k in range(2):
            o = C_DM + (HEADS * k + h) * NMETA
            c[:NMETA, o:o + NMETA] = -np.abs(m[:, None] - m[None, :]) * SLOPES[h] / SCALE
    c[:, C_IOTA:C_IOTA + P] = i
    c[:, C_PG:C_PG + NG] = NG - np.arange(NG)
    c[:, C_PE:C_PE + NE] = NE - np.arange(NE)
    for t in range(4):
        c[:, C_ROW + t] = P * t + i - FAR
        c[:, C_ROW + 4 + t] = P * t + i - FAR + NTOK
        c[:, C_VALID + t] = i < TN[t]
    for g, w in enumerate(WINDOWS):
        c[:, C_POOL + NMETA * g:C_POOL + NMETA * (g + 1)] = w / np.minimum(m + 1, w)
    c[:, C_HALF] = -0.5
    return c


UNITS = [(kind, h) for h in range(HEADS) for kind in ("frames1", "frames0")]
UNITS += [("decode", h) for h in range(HEADS)] + [("meta", 0)]
STEPS = len(UNITS) + 2


def transposed_tasks():
    out = [("state", 0, "act")]
    for j in range(STEPS):
        if j < 8:
            out += [("cachek", j, "dve"), ("past", j, "dve")]
            if j < 4:
                out.append(("k", j, "act"))
        if 1 <= j <= 8:
            out.append(("vu", j - 1, "act"))
        if j >= 2:
            out.append(("w", j - 2, "dve"))
    return out


TASKS = transposed_tasks()
TASK = {(kind, n): i for i, (kind, n, _) in enumerate(TASKS)}
N_TASK = len(TASKS)
N_ACT = sum(e == "act" for _, _, e in TASKS)
N_DVE = N_TASK - N_ACT


def emptied(l, i):
    e = TASKS[i][2]
    n = sum(x[2] == e for x in TASKS[:i + 1])
    return e, l * (N_ACT if e == "act" else N_DVE) + n


def program(nc, t, o):
    ctx = ExitStack()
    with ctx:
        def sb(name, shape, dt=F32):
            return ctx.enter_context(nc.sbuf_tensor(name, shape, dt))

        def sem(name):
            return ctx.enter_context(nc.semaphore(name))

        PS = ctx.enter_context(nc.psum_tensor("PS", [P, 8, 512], F32))
        ring = sb("ring", [P, SLOTS, CH])
        H = sb("H", [P, 4, D])
        FT = sb("FT", [P, KT, NTOK])
        qT = sb("qT", [P, HEADS, NTOK])
        kT = sb("kT", [P, HEADS, NTOK])
        CT = sb("CT", [P, C_END - 0])
        M = sb("M", [P, 7216])
        N = sb("N", [P, 5608])
        D4 = sb("D4", [P, 4, NTOK])
        qz = sb("qz", [P, HEADS, DB, 2, DS])
        wpool = sb("wpool", [P, 4, P])
        cols = sb("cols", [P, 16])
        lam = sb("lam", [P, 8])
        stats = sb("stats", [P, 4, 16])
        gates = sb("gates", [P, 2, 4])
        idx = sb("idx", [P, 2, NE], U32)
        more_rounds = sb("more_rounds", [1, 1], I32)

        ident, tri, ones = (CT[:, c:c + P] for c in (C_ID, C_TRI, C_ONE))
        ckv = [M[:, 512 * i:512 * i + 512] for i in range(4)]
        kout = M[:, 2048:2560].rearrange("p (t e) -> p t e", t=4)
        OT = M[:, 2560:4160].rearrange("p (h n) -> p h n", h=HEADS)
        uout = M[:, 4160:4416].rearrange("p (t e) -> p t e", t=2)
        V = M[:, 4416:6464].rearrange("p (t n) -> p t n", t=4)
        Wt = M[:, 6464:6736]
        stT = M[:, 6736:7216].rearrange("p (g n) -> p g n", g=4)
        pr = [N[:, 544 * i:544 * i + 544].rearrange("p (m n) -> p m n", m=2) for i in range(2)]
        WT = [N[:, 1088 + 384 * i:1472 + 384 * i].rearrange("p (k q) -> p k q", k=3) for i in range(2)]
        ST = N[:, 1856:2880].rearrange("p (h m q) -> p h m q", h=HEADS, m=2)
        kct = N[:, 2880:3392].rearrange("p (h k) -> p h k", h=HEADS)
        WTp = N[:, 3392:3904].rearrange("p (h q) -> p h q", h=HEADS)
        EXT = STATE + NMETA + SEQ
        EW = EXT + DB * (STATE + DS)
        ue, wa, wb = (N[:, 3904 + EW * i:3904 + EW * (i + 1)] for i in range(3))
        spin, vT = wa[:, 0:512], wb[:, 0:NTOK]
        small = N[:, 5512:5608]
        RT = [N[:, 64 * i:64 * i + 64].rearrange("p (t e) -> p t e", t=4) for i in range(14)]
        lgT = N[0:NE, 900:1300]
        hot = [N[:, 1300 + 512 * k:1812 + 512 * k].rearrange("p (t s) -> p t s", t=4) for k in range(2)]
        vals = N[:, 2324:2580].rearrange("p (k t n) -> p k t n", k=2, t=4)
        r4 = [N[:, 2580 + 4 * i:2584 + 4 * i] for i in range(12)]
        pairs6 = N[:, 2640:2736].rearrange("p (t g n) -> p t g n", t=4, g=4)
        g4 = [N[:, 2736 + 16 * i:2752 + 16 * i].rearrange("p (t g) -> p t g", t=4) for i in range(4)]
        rw = sb("rw", [P, KT, NE])
        rb_ = sb("rb_", [P, NE])
        xg = [M[:, 1024 * i:1024 * i + 1024] for i in range(2)]
        xgT = [M[:, 2048 + 1024 * i:3072 + 1024 * i].rearrange("p (k s) -> p k s", k=KT) for i in range(2)]
        ob = [M[:, 4096 + 1024 * i:5120 + 1024 * i] for i in range(2)]
        hid = M[:, 6144:6656]
        hidT = M[:, 6656:7168].rearrange("p (k s) -> p k s", k=4)
        yb = [M[:, 2048 * i:2048 * i + 2048].rearrange("p (k n) -> p k n", k=2) for i in range(2)]
        gb = M[:, 4096:6144].rearrange("p (k n) -> p k n", k=2)
        lq = M[:, 0:512].rearrange("p (l n) -> p l n", l=DEPTH)

        xs = nc.dram_tensor("xs", (NTOK, D), F32, kind="Internal").ap()
        ys = nc.dram_tensor("ys", (2 * NTOK, D), F32, kind="Internal").ap()
        us = nc.dram_tensor("us", (DEPTH, DB, DS, AW), F32, kind="Internal").ap()

        landed = [sem(f"slot_landed{s}") for s in range(SLOTS)]
        x_in, consts_in, cols_in, gb_in = sem("x_in"), sem("consts_in"), sem("cols_in"), sem("gb_in")
        ckv_in = [sem(f"ckv_in{i}") for i in range(4)]
        state_in, wpool_in = sem("state_in"), sem("wpool_in")
        lam_sum, lam_exp, lam_done, qz_zero = sem("lam_sum"), sem("lam_exp"), sem("lam_done"), sem("qz_zero")
        dve_step, pool_step, act_step = sem("dve_step"), sem("pool_step"), sem("act_step")
        ln_var, ln_rstd, ln_scaled, ln_out = sem("ln_var"), sem("ln_rstd"), sem("ln_scaled"), sem("ln_out")
        hx_ps, hx_dve, hx_act = sem("hx_ps"), sem("hx_dve"), sem("hx_act")
        proj_ps, proj_sb, qz_done = sem("proj_ps"), sem("proj_sb"), sem("qz_done")
        task_ps, task_act, task_dve = sem("task_ps"), sem("task_act"), sem("task_dve")
        score_ps, score_max, exp_done, w_done = sem("score_ps"), sem("score_max"), sem("exp_done"), sem("w_done")
        av_ps, ot_sb = sem("av_ps"), sem("ot_sb")
        cv_used = sem("cv_used")
        d4_done, pm_ps, pm_sb = sem("d4_done"), sem("pm_ps"), sem("pm_sb")
        sq_done, ss_ps, rms_done, mix_done = sem("sq_done"), sem("ss_ps"), sem("rms_done"), sem("mix_done")
        k_out, v_out, u_out, us_out = sem("k_out"), sem("v_out"), sem("u_out"), sem("us_out")
        op_ps, res_done = sem("op_ps"), sem("res_done")
        xs_out = sem("xs_out")
        lg_ps, lg_sb, lgt_ps, hot_done, rank_ps, idx_in, idx_ps, idx_ready, routed = (
            sem("lg_ps"), sem("lg_sb"), sem("lgt_ps"), sem("hot_done"), sem("rank_ps"), sem("idx_in"), sem("idx_ps"),
            sem("idx_ready"), sem("routed"))
        xg_in = [sem(f"xg_in{i}") for i in range(2)]
        xg_zero = sem("xg_zero")
        xt_ps, xt_dve, xt_act = sem("xt_ps"), sem("xt_dve"), sem("xt_act")
        gate_ps, up_ps, silu_done, hid_done = sem("gate_ps"), sem("up_ps"), sem("silu_done"), sem("hid_done")
        ht_ps, ht_sb = sem("ht_ps"), sem("ht_sb")
        o_ps, o_dve, o_act = sem("o_ps"), sem("o_dve"), sem("o_act")
        scat = [sem(f"scattered{i}") for i in range(2)]
        round_closed = sem("round_closed")
        y_in = [sem(f"y_in{i}") for i in range(2)]
        comb = sem("combined")
        y_out = sem("y_out")
        lg_shifted, rank_moved = sem("lg_shifted"), sem("rank_moved")
        pool_past_wait = sem("pool_past_wait")

        block = ctx.enter_context(nc.Block())

        def dense_use(l, rb):
            return l + PAIRS * rb

        def round_use(l, rb, r):
            return l + 1 + PAIRS * (rb + r)

        LN1 = [1, 3]
        LN2 = [2, 4]

        @block.sync
        def _(sp):
            def load(s, view):
                n = view.shape[-1]
                sp.dma_start(ring[:, s, :].rearrange("p (k n) -> p k n", n=n), view).then_inc(landed[s], 16)

            def expert(w, l, e):
                return w[l, bass.ds(e, 1), :, :].rearrange("o (k p) n -> p (o k) n", p=P)

            def load_up(l, e, s, E, dense):
                for n, (w, used, was) in enumerate((("w_gate", gate_ps, dense[0]), ("w_up", up_ps, dense[1]))):
                    if was is None:
                        sp.wait_ge(used, E - 1)
                    else:
                        sp.wait_ge(*was)
                    load(s + n, expert(t[w], l, e))

            def load_down(l, e, s, E, was):
                if was is None:
                    sp.wait_ge(o_ps, 2 * E - 2)
                else:
                    sp.wait_ge(*was)
                load(s, expert(t["w_down"], l, e))

            def round_(l, E0, first_round):
                d = [(proj_ps, 16 * l + 4), (proj_ps, 16 * l + 8), (proj_ps, 16 * l + 12), (proj_ps, 16 * l + 16),
                     (op_ps, 4 * l + 4), (op_ps, 4 * l + 4)] if first_round else [None] * SLOTS
                load_up(l, 0, 0, E0, d[0:2])
                load_up(l, 1, 3, E0 + 1, d[3:5])
                load_down(l, 0, 5, E0, d[5])
                load_up(l, 2, 0, E0 + 2, [None] * 2)
                load_down(l, 1, 2, E0 + 1, d[2])
                load_up(l, 3, 3, E0 + 3, [None] * 2)
                load_down(l, 2, 5, E0 + 2, None)
                with sp.Fori(2, PAIRS) as i:
                    e = 2 * i
                    load_up(l, e, 0, E0 + e, [None] * 2)
                    load_down(l, e - 1, 2, E0 + e - 1, None)
                    load_up(l, e + 1, 3, E0 + e + 1, [None] * 2)
                    load_down(l, e, 5, E0 + e, None)
                load_down(l, NE - 1, 2, E0 + NE - 1, None)

            rb = 0
            for l in range(DEPTH):
                if l > 0:
                    last = [(gate_ps, 16 * more + 15), (up_ps, 16 * more + 15), (o_ps, 32 * rb), (gate_ps, 16 * rb),
                            (up_ps, 16 * rb), (o_ps, 32 * more + 30)]
                for s in (0, 1, 3, 4, 5, 2) if l > 0 else range(SLOTS):
                    w, c = ("w_in", s) if s < 4 else ("w_out", s - 4)
                    if l > 0:
                        sp.wait_ge(*last[s])
                    load(s, t[w][l, :, c * 512:(c + 1) * 512].rearrange("(k p) n -> p k n", p=P))
                round_(l, 16 * rb, True)
                sp.wait_ge(routed, l + 1)
                more = sp.value_load(more_rounds[0:1, 0:1], min_val=0, max_val=3)
                R = more + 1
                with sp.If(more > 0):
                    with sp.Fori(1, R) as r:
                        round_(l, 16 * (rb + r), False)
                rb = rb + R

        @block.tensor
        def _(pe):
            def chunk(s, use):
                pe.wait_ge(landed[s], 16 * (use + 1))

            def turn_h(q):
                for j in range(4):
                    n = 4 * q + j
                    pe.wait_ge(ln_out, n + 1)
                    if n >= 2:
                        pe.wait_ge(hx_dve, n - 1)
                        pe.wait_ge(hx_act, n - 1)
                    for half in range(2):
                        bank = 2 + 2 * (j % 2) + half
                        for k in range(4):
                            mm = pe.transpose(PS[:, bank, k * P:k * P + TN[j]],
                                              H[0:TN[j], j, (4 * half + k) * P:(4 * half + k + 1) * P],
                                              ident[0:TN[j], 0:TN[j]])
                        mm.then_inc(hx_ps, 1)

            def task_bank(l, i):
                if i >= 2:
                    e, n = emptied(l, i - 2)
                    pe.wait_ge(task_act if e == "act" else task_dve, n)
                return 4 + i % 2

            def proj(l, m, use):
                s = m // 4
                if m % 4 == 0:
                    chunk(s, use)
                if m >= 2:
                    pe.wait_ge(proj_sb, 16 * l + m - 1)
                w = ring[:, s, :].rearrange("p (k n) -> p k n", k=KT)
                for k in range(KT):
                    mm = pe.matmul(PS[:, m % 2, 0:NTOK], w[:, k, (m % 4) * P:(m % 4 + 1) * P], FT[:, k, :],
                                   start=(k == 0), stop=(k == KT - 1))
                mm.then_inc(proj_ps, 1)

            def scores(l, i):
                kind, h = UNITS[i]
                if i >= 1:
                    pe.wait_ge(score_max, 13 * l + i)
                for m in range(2):
                    r = slice(64 * m, 64 * m + 64)
                    if kind in ("frames1", "frames0"):
                        q0, n = (TC[1], 272) if kind == "frames1" else (TC[0], 144)
                        mm = pe.matmul(PS[:, 2 + m, 0:n], qT[r, h, q0:q0 + P], kT[r, h, 0:n], start=True, stop=True)
                    elif kind == "decode":
                        pe.transpose(PS[:, 2 + m, 0:P], ST[:, h, m, :], ident)
                        mm = pe.matmul(PS[:, 2 + m, P:2 * P], qT[r, h, DEC:NTOK], kT[r, h, DEC:NTOK],
                                       start=True, stop=True)
                    else:
                        for g in range(HEADS):
                            c = g * NMETA
                            mm = pe.matmul(PS[0:NMETA, 2 + m, c:c + NMETA], qT[r, g, 0:NMETA], kT[r, g, 0:NMETA],
                                           start=True, stop=True)
                mm.then_inc(score_ps, 1)

            def w_blocks(l, i):
                kind, h = UNITS[i]
                n = TASK["w", i]
                bank = task_bank(l, n)
                pe.wait_ge(w_done, 13 * l + i + 1)
                if kind == "frames1" or kind == "frames0":
                    nb = 2 if kind == "frames1" else 1
                    for k in range(nb):
                        pe.transpose(PS[:, bank, k * P:(k + 1) * P], Wt[:, NMETA + k * P:NMETA + (k + 1) * P], ident)
                    mm = pe.transpose(PS[0:NMETA, bank, nb * P:(nb + 1) * P], Wt[:, 0:NMETA], ident)
                elif kind == "decode":
                    for k in range(2):
                        mm = pe.transpose(PS[:, bank, k * P:(k + 1) * P], Wt[:, k * P:(k + 1) * P], ident)
                else:
                    for g in range(HEADS):
                        mm = pe.transpose(PS[0:NMETA, bank, g * NMETA:(g + 1) * NMETA],
                                          Wt[0:NMETA, g * NMETA:(g + 1) * NMETA], ident[0:NMETA, 0:NMETA])
                mm.then_inc(task_ps, 1)

            def av(l, i):
                kind, h = UNITS[i]
                e, n = emptied(l, TASK["w", i])
                pe.wait_ge(task_dve, n)
                wt = WT[i % 2]
                hs = slice(h * P, (h + 1) * P)
                if kind in ("frames1", "frames0"):
                    _, n = emptied(l, TASK["vu", h])
                    pe.wait_ge(task_act, n)
                    if i >= 2:
                        pe.wait_ge(ot_sb, 10 * l + i - 1)
                    nb = 2 if kind == "frames1" else 1
                    out = PS[:, 6 + i % 2, 0:P]
                    for k in range(nb):
                        pe.matmul(out, V[:, k, hs], wt[:, k, :], start=(k == 0), stop=False)
                    mm = pe.matmul(out, V[0:NMETA, 3, hs], wt[0:NMETA, nb, :], start=False, stop=True)
                    mm.then_inc(av_ps, 1)
                elif kind == "decode":
                    if h == 0:
                        pe.wait_ge(proj_sb, 16 * l + 15)
                    pe.matmul(PS[:, 0, hs], V[:, 2, hs], wt[:, 1, :], start=(h == 0), stop=False,
                              skip_group_check=True)
                else:
                    pe.wait_ge(proj_sb, 16 * l + 16)
                    wm = wt[0:NMETA, 0, 0:HEADS * NMETA].rearrange("p (g q) -> p g q", g=HEADS)
                    for g in range(HEADS):
                        mm = pe.matmul(PS[:, 1, g * NMETA:(g + 1) * NMETA], V[0:NMETA, 3, g * P:(g + 1) * P],
                                       wm[:, g, :], start=True, stop=True)
                    mm.then_inc(av_ps, 1)

            def attention(l, use):
                for m in range(8):
                    proj(l, m, use)
                n = TASK["state", 0]
                bank = task_bank(l, n) if n >= 2 else 4
                pe.wait_ge(state_in, 16 * (l + 1))
                for g in range(4):
                    mm = pe.transpose(PS[:, bank, g * 120:(g + 1) * 120], spin[0:120, g * P:(g + 1) * P],
                                      ident[0:120, 0:120])
                mm.then_inc(task_ps, 1)
                pe.wait_ge(proj_sb, 16 * l + 8)
                for j in range(STEPS):
                    if j < 8:
                        bank = task_bank(l, TASK["cachek", j])
                        pe.wait_ge(ckv_in[j % 4], 16 * (4 * l + j // 4 + 1))
                        for h in range(HEADS):
                            mm = pe.transpose(PS[:, bank, h * P:(h + 1) * P], ckv[j % 4][:, h * P:(h + 1) * P], ident)
                        mm.then_inc(task_ps, 1)
                        proj(l, 8 + j, use)
                        bank = task_bank(l, TASK["past", j])
                        pe.wait_ge(task_dve, emptied(l, TASK["cachek", j])[1])
                        if j == 0:
                            pe.wait_ge(qz_done, l + 1)
                        for h in range(HEADS):
                            mm = pe.matmul(PS[:, bank, h * 32:(h + 1) * 32], kct[:, h, :],
                                           qz[:, h, j, :, :].rearrange("p m t -> p (m t)"), start=True, stop=True)
                        mm.then_inc(task_ps, 1)
                        if j < 4:
                            bank = task_bank(l, TASK["k", j])
                            for x in range(4):
                                mm = pe.transpose(PS[0:TN[x], bank, x * P:(x + 1) * P],
                                                  kT[:, j, TC[x]:TC[x] + TN[x]], ident)
                            mm.then_inc(task_ps, 1)
                    if 1 <= j <= 8:
                        n = j - 1
                        bank = task_bank(l, TASK["vu", n])
                        pe.wait_ge(proj_sb, 16 * l + 9 + n)
                        tiles = range(4) if n < 4 else (1, 2)
                        src = vT if n < 4 else D4[:, n - 4, :]
                        for y, x in enumerate(tiles):
                            mm = pe.transpose(PS[0:TN[x], bank, y * P:(y + 1) * P], src[:, TC[x]:TC[x] + TN[x]],
                                              ident)
                        mm.then_inc(task_ps, 1)
                    if j < len(UNITS):
                        if UNITS[j][0] == "decode":
                            pe.wait_ge(task_dve, emptied(l, TASK["past", 7])[1])
                        scores(l, j)
                    if j >= 2:
                        w_blocks(l, j - 2)
                        av(l, j - 2)
                for g in range(4):
                    if g == 0:
                        pe.wait_ge(ot_sb, 10 * l + 8)
                        if l == 0:
                            pe.wait_ge(wpool_in, 16)
                        else:
                            pe.wait_ge(wpool_in, 32)
                    if g >= 2:
                        pe.wait_ge(pm_sb, 4 * l + g - 1)
                    pe.wait_ge(d4_done, 4 * l + g + 1)
                    pe.matmul(PS[:, 6 + g % 2, 0:NTOK], wpool[:, g, :], D4[:, g, :], start=True,
                              stop=True).then_inc(pm_ps, 1)
                for b in range(DB):
                    pe.wait_ge(ckv_in[b % 4], 16 * (4 * l + 2 + b // 4 + 1))
                    for h in range(HEADS):
                        c = h * P + b * DS
                        mm = pe.matmul(PS[:, 0, c:c + DS], ckv[b % 4][:, h * P:(h + 1) * P],
                                       WTp[:, h, b * DS:(b + 1) * DS], start=False, stop=(b == DB - 1 and h == 3),
                                       skip_group_check=True)
                    mm.then_inc(cv_used, 1)
                for h in range(HEADS):
                    pe.wait_ge(sq_done, 4 * l + h + 1)
                    if h == 0:
                        pe.wait_ge(score_max, 13 * l + 13)
                    if h == 2:
                        pe.wait_ge(task_dve, (l + 1) * N_DVE)
                        pe.wait_ge(task_act, (l + 1) * N_ACT)
                    pe.matmul(PS[:, 2 + h, 0:NTOK], ones, FT[:, h, :], start=True, stop=True).then_inc(ss_ps, 1)

            def out_proj(l, use):
                pe.wait_ge(mix_done, 4 * (l + 1))
                pe.wait_ge(pm_sb, 4 * (l + 1))
                pe.wait_ge(ot_sb, 10 * (l + 1))
                for j in range(4):
                    if j >= 2:
                        pe.wait_ge(res_done, 4 * l + j - 1)
                    for half in range(2):
                        if j == 0:
                            chunk(4 + half, use)
                        w = ring[:, 4 + half, :].rearrange("p (k n) -> p k n", k=KT)
                        for k in range(KT):
                            mm = pe.matmul(PS[0:TN[j], 6 * (j % 2) + half, :], FT[:, k, TC[j]:TC[j] + TN[j]],
                                           w[:, k, :], start=(k == 0), stop=(k == KT - 1))
                    mm.then_inc(op_ps, 1)

            def route(l):
                for j in range(4):
                    pe.wait_ge(hx_dve, 4 * LN1[l] + j + 1)
                    pe.wait_ge(hx_act, 4 * LN1[l] + j + 1)
                for k in range(KT):
                    mm = pe.matmul(PS[0:NE, 0, 0:NTOK], rw[:, k, :], FT[:, k, :], start=(k == 0), stop=(k == KT - 1))
                mm.then_inc(lg_ps, 1)
                pe.wait_ge(lg_sb, l + 1)
                for j in range(4):
                    mm = pe.transpose(PS[0:TN[j], 1, j * NE:(j + 1) * NE], lgT[:, TC[j]:TC[j] + TN[j]],
                                      ident[0:NE, 0:NE])
                mm.then_inc(lgt_ps, 1)
                pe.wait_ge(hot_done, l + 1)
                pe.matmul(PS[:, 2, 0:64], tri, RT[13].rearrange("p t e -> p (t e)"), start=True, stop=True)
                pe.matmul(PS[:, 3, 0:64], ones, RT[13].rearrange("p t e -> p (t e)"), start=True,
                          stop=True).then_inc(rank_ps, 1)

            def moe_round(l, rb, r):
                base = round_use(l, rb, r)

                def turn_x(i, par):
                    E = 16 * (rb + r) + 2 * i + par
                    pe.wait_ge(xg_in[par], 16 * (PAIRS * (rb + r) + i + 1))
                    if not (isinstance(i, int) and i == 0 and par == 0):
                        pe.wait_ge(xt_dve, E)
                        pe.wait_ge(xt_act, E)
                    for half in range(2):
                        for k in range(4):
                            mm = pe.transpose(PS[:, 2 + half, k * P:(k + 1) * P],
                                              xg[par][:, (4 * half + k) * P:(4 * half + k + 1) * P], ident)
                        mm.then_inc(xt_ps, 1)

                def up(i, par, first):
                    E = 16 * (rb + r) + 2 * i + par
                    pe.wait_ge(xt_dve, E + 1)
                    pe.wait_ge(xt_act, E + 1)
                    if not first:
                        pe.wait_ge(hid_done, E)
                    for n in range(2):
                        s = 3 * par + n
                        chunk(s, base + i)
                        w = ring[:, s, :].rearrange("p (k n) -> p k n", k=KT)
                        for k in range(KT):
                            mm = pe.matmul(PS[:, n, :], xgT[par][:, k, :], w[:, k, :], start=(k == 0),
                                           stop=(k == KT - 1))
                        mm.then_inc(gate_ps if n == 0 else up_ps, 1)

                def turn_hid(i, par, first):
                    E = 16 * (rb + r) + 2 * i + par
                    pe.wait_ge(hid_done, E + 1)
                    if not first:
                        pe.wait_ge(ht_sb, E)
                    for k in range(4):
                        mm = pe.transpose(PS[:, 4, k * P:(k + 1) * P], hid[:, k * P:(k + 1) * P], ident)
                    mm.then_inc(ht_ps, 1)

                def down(i, par, first):
                    E = 16 * (rb + r) + 2 * i + par
                    s = 5 if par == 0 else 2
                    chunk(s, base + i)
                    pe.wait_ge(ht_sb, E + 1)
                    if not first:
                        pe.wait_ge(o_dve, E)
                        pe.wait_ge(o_act, E)
                    w = ring[:, s, :].rearrange("p (k n) -> p k n", k=4)
                    for half in range(2):
                        for k in range(4):
                            mm = pe.matmul(PS[:, 5 + half, :], hidT[:, k, :], w[:, k, half * 512:(half + 1) * 512],
                                           start=(k == 0), stop=(k == 3))
                        mm.then_inc(o_ps, 1)

                def pair(i, first, last):
                    up(i, 0, first)
                    turn_x(i, 1)
                    if not first:
                        down(i - 1, 1, False)
                    turn_hid(i, 0, first)
                    up(i, 1, False)
                    if not last:
                        turn_x(i + 1, 0)
                    down(i, 0, first)
                    turn_hid(i, 1, False)

                pe.wait_ge(idx_in, rb + r + 1)
                for k in range(2):
                    for j in range(4):
                        mm = pe.matmul(PS[:, 7, 0:2 * NE], hot[k][:, j, :], vals[:, k, j, :],
                                       start=(k == 0 and j == 0), stop=(k == 1 and j == 3))
                mm.then_inc(idx_ps, 1)
                turn_x(0, 0)
                pair(0, True, False)
                with pe.Fori(1, PAIRS - 1) as i:
                    pair(i, False, False)
                pair(PAIRS - 1, False, True)
                down(PAIRS - 1, 1, False)

            pe.wait_ge(consts_in, 16)
            turn_h(0)
            rb = 0
            for l in range(DEPTH):
                if l > 0:
                    turn_h(LN2[l - 1])
                for j in range(4):
                    pe.wait_ge(hx_dve, 4 * LN2[l - 1] + j + 1 if l else j + 1)
                    pe.wait_ge(hx_act, 4 * LN2[l - 1] + j + 1 if l else j + 1)
                use = dense_use(l, rb)
                attention(l, use)
                out_proj(l, use)
                turn_h(LN1[l])
                route(l)
                pe.wait_ge(routed, l + 1)
                more = pe.value_load(more_rounds[0:1, 0:1], min_val=0, max_val=3)
                R = more + 1
                with pe.Fori(0, R) as r:
                    moe_round(l, rb, r)
                rb = rb + R

        @block.vector
        def _(dve):
            steps = [0]

            def did(ins):
                steps[0] += 1
                ins.then_inc(dve_step, 1)
                return steps[0]

            def after(n):
                dve.wait_ge(dve_step, n)

            def then(ins):
                after(did(ins))

            def ln_front(q, j):
                n = TN[j]
                st = stats[0:n, j, :]
                for half in range(2):
                    c = did(dve.bn_stats(st[:, 6 * half:6 * half + 6], H[0:n, j, half * 512:(half + 1) * 512]))
                after(c)
                then(dve.bn_aggr(st[:, 12:14], st[:, 0:12]))
                dve.tensor_scalar(st[:, 14:15], st[:, 13:14], EPS, None, ALU.add).then_inc(ln_var, 1)

            def ln_back(q, j):
                n = TN[j]
                st = stats[0:n, j, :]
                if j == 0:
                    dve.wait_ge(gb_in, 32 * (q + 1))
                dve.wait_ge(ln_rstd, 4 * q + j + 1)
                then(dve.tensor_scalar(H[0:n, j, :], H[0:n, j, :], st[:, 12:13], st[:, 15:16], ALU.subtract,
                                       ALU.mult))
                dve.tensor_tensor(H[0:n, j, :], H[0:n, j, :], gb[0:n, 0, :], ALU.mult).then_inc(ln_scaled, 1)

            def turn_h(q):
                for j in range(4):
                    bank = 2 + 2 * (j % 2)
                    dve.wait_ge(hx_ps, 8 * q + 2 * j + 1)
                    dve.tensor_copy(FT[:, 0:4, TC[j]:TC[j] + TN[j]],
                                    PS[:, bank, :].rearrange("p (k n) -> p k n", k=4)[:, :, 0:TN[j]]
                                    ).then_inc(hx_dve, 1)

            def front(l, i):
                kind, h = UNITS[i]
                x = pr[i % 2]
                dve.wait_ge(score_ps, 13 * l + i + 1)
                if i >= 2:
                    dve.wait_ge(dve_step, w_read[i - 2])
                sm = small[:, 12 * (i % 4):12 * (i % 4) + 12]
                if kind == "meta":
                    xm = x[0:NMETA].rearrange("p m n -> p (m n)")[:, 0:128].rearrange("p (g n) -> p g n", g=8)
                    mx = small[0:NMETA, 48:56]
                    then(dve.tensor_tensor(xm.rearrange("p (m h) n -> p m (h n)", m=2), PS[0:NMETA, 2:4, 0:64],
                                           CT[0:NMETA, C_DM:C_DM + 128].rearrange("p (m n) -> p m n", m=2), ALU.add))
                    then(dve.tensor_reduce(mx, xm, X, ALU.max))
                    dve.tensor_tensor(xm, xm, mx.unsqueeze(2).broadcast_to([NMETA, 8, NMETA]),
                                      ALU.subtract).then_inc(score_max, 1)
                    return
                col, n = {"frames1": (C_D1, 272), "frames0": (C_D0, 144), "decode": (C_DD, 256)}[kind]
                then(dve.scalar_tensor_tensor(x[:, :, 0:n], CT[:, col:col + n].unsqueeze(1).broadcast_to([P, 2, n]),
                                              SLOPES[h] / SCALE, PS[:, 2:4, 0:n], ALU.mult, ALU.add))
                then(dve.tensor_reduce(sm[:, 0:2], x[:, :, 0:n], X, ALU.max))
                dve.tensor_scalar(sm[:, 2:4], sm[:, 0:2], -SCALE, None, ALU.mult).then_inc(score_max, 1)

            def back(l, i):
                kind, h = UNITS[i]
                x = pr[i % 2]
                dve.wait_ge(exp_done, 13 * l + i + 1)
                if i >= 1:
                    dve.wait_ge(task_ps, l * N_TASK + TASK["w", i - 1] + 1)
                sm = small[:, 12 * (i % 4):12 * (i % 4) + 12]
                if kind == "meta":
                    xm = x[0:NMETA].rearrange("p m n -> p (m n)")[:, 0:128].rearrange("p (g n) -> p g n", g=8)
                    s = small[0:NMETA, 56:64]
                    then(dve.tensor_reduce(s, xm, X, ALU.add))
                    then(dve.reciprocal(small[0:NMETA, 64:72], s))
                    x2 = small[0:NMETA, 68:72]
                    then(dve.tensor_scalar(x2, x2, lam[0:NMETA, l:l + 1], None, ALU.mult))
                    then(dve.tensor_tensor(xm, xm, small[0:NMETA, 64:72].unsqueeze(2).broadcast_to([NMETA, 8, NMETA]),
                                           ALU.mult))
                    w_read[i] = did(dve.tensor_tensor(
                        Wt[0:NMETA, 0:64].rearrange("p (h n) -> p h n", h=HEADS), xm[:, 0:4, :], xm[:, 4:8, :],
                        ALU.add))
                else:
                    n = {"frames1": 272, "frames0": 144, "decode": 256}[kind]
                    then(dve.reciprocal(sm[:, 6:8], sm[:, 4:6]))
                    c = did(dve.tensor_scalar(sm[:, 8:9], sm[:, 7:8], lam[:, l:l + 1], None, ALU.mult))
                    c = did(dve.tensor_scalar(Wt[:, 0:n], x[:, 0, 0:n], sm[:, 6:7], None, ALU.mult))
                    after(c)
                    w_read[i] = did(dve.scalar_tensor_tensor(Wt[:, 0:n], x[:, 1, 0:n], sm[:, 8:9], Wt[:, 0:n],
                                                             ALU.mult, ALU.add))
                after(w_read[i])
                dve.sem_inc(w_done, 1)

            def task(l, kind, n):
                i = TASK[kind, n]
                bank = 4 + i % 2
                dve.wait_ge(task_ps, l * N_TASK + i + 1)
                if kind == "cachek":
                    dve.tensor_copy(kct.rearrange("p h k -> p (h k)"), PS[:, bank, :]).then_inc(task_dve, 1)
                elif kind == "past":
                    dve.tensor_copy(ST[:, :, :, n * DS:(n + 1) * DS],
                                    PS[:, bank, 0:128].rearrange("p (h m t) -> p h m t", h=HEADS, m=2)
                                    ).then_inc(task_dve, 1)
                else:
                    what, h = UNITS[n]
                    wt = WT[n % 2]
                    if what in ("frames1", "frames0"):
                        nb = 2 if what == "frames1" else 1
                        dve.tensor_copy(wt[:, 0:nb, :], PS[:, bank, 0:nb * P].rearrange("p (k q) -> p k q", k=nb))
                        dve.tensor_copy(wt[0:NMETA, nb, :], PS[0:NMETA, bank, nb * P:(nb + 1) * P]
                                        ).then_inc(task_dve, 1)
                    elif what == "decode":
                        dve.tensor_copy(WTp[:, h, :], PS[:, bank, 0:P])
                        dve.tensor_copy(wt[:, 1, :], PS[:, bank, P:2 * P]).then_inc(task_dve, 1)
                    else:
                        dve.tensor_copy(wt[0:NMETA, 0, 0:64], PS[0:NMETA, bank, 0:64]).then_inc(task_dve, 1)

            def route(l):
                lg, pb, sel, t0, t1, oh1, oh2, rk = RT[0:8]
                mask = RT[13]

                def tt(out, a, b, op):
                    then(dve.tensor_tensor(out, a, b, op))

                def ts(out, a, s1, s2, o1, o2=None):
                    then(dve.tensor_scalar(out, a, s1, s2, o1, o2) if o2 is not None
                         else dve.tensor_scalar(out, a, s1, s2, o1))

                def red(out, a, op):
                    then(dve.tensor_reduce(out, a, X, op))

                def wide(a, n=NE):
                    return a.unsqueeze(2).broadcast_to([P, 4, n])

                pri = CT[:, C_PE:C_PE + NE].unsqueeze(1).broadcast_to([P, 4, NE])
                prig = CT[:, C_PG:C_PG + NG].unsqueeze(1).broadcast_to([P, 4, NG])
                valid = CT[:, C_VALID:C_VALID + 4]
                dve.wait_ge(lg_ps, l + 1)
                dve.tensor_copy(lgT, PS[0:NE, 0, 0:NTOK]).then_inc(lg_sb, 1)
                then(dve.memset(lg, 0.0))
                dve.wait_ge(lgt_ps, l + 1)
                c = did(dve.tensor_copy(lg[:, 0:3, :], PS[:, 1, 0:48].rearrange("p (t e) -> p t e", t=3)))
                c = did(dve.tensor_copy(lg[0:NMETA, 3, :], PS[0:NMETA, 1, 48:64]))
                after(c)
                red(r4[0], lg, ALU.max)
                dve.tensor_tensor(lg, lg, wide(r4[0]), ALU.subtract).then_inc(lg_shifted, 1)
                dve.wait_ge(act_step, l + 1)
                red(r4[1], lg, ALU.add)
                then(dve.reciprocal(r4[2], r4[1]))
                tt(pb, lg, wide(r4[2]), ALU.mult)
                tt(sel, pb, rb_[:, :].unsqueeze(1).broadcast_to([P, 4, NE]), ALU.add)
                s4 = sel.rearrange("p t (g e) -> p t g e", g=NG)
                c = did(dve.tensor_tensor(pairs6[:, :, :, 0:3], s4[:, :, :, 0:3], s4[:, :, :, 1:4], ALU.add))
                c = did(dve.tensor_tensor(pairs6[:, :, :, 3:5], s4[:, :, :, 0:2], s4[:, :, :, 2:4], ALU.add))
                c = did(dve.tensor_tensor(pairs6[:, :, :, 5:6], s4[:, :, :, 0:1], s4[:, :, :, 3:4], ALU.add))
                after(c)
                red(g4[0], pairs6, ALU.max)
                red(r4[3], g4[0], ALU.max)
                tt(g4[1], g4[0], wide(r4[3], NG), ALU.is_ge)
                tt(g4[2], g4[1], prig, ALU.mult)
                red(r4[4], g4[2], ALU.max)
                tt(g4[3], g4[2], wide(r4[4], NG), ALU.is_equal)
                gw = g4[3].unsqueeze(3).broadcast_to([P, 4, NG, EPG])
                then(dve.tensor_tensor(t0.rearrange("p t (g e) -> p t g e", g=NG), s4, gw, ALU.mult))
                ts(g4[2], g4[3], 1.0, -NEG, ALU.subtract, ALU.mult)
                gw = g4[2].unsqueeze(3).broadcast_to([P, 4, NG, EPG])
                t04 = t0.rearrange("p t (g e) -> p t g e", g=NG)
                then(dve.tensor_tensor(t04, t04, gw, ALU.add))
                for n, oh in ((0, oh1), (1, oh2)):
                    red(r4[5], t0, ALU.max)
                    tt(t1, t0, wide(r4[5]), ALU.is_ge)
                    tt(t1, t1, pri, ALU.mult)
                    red(r4[6], t1, ALU.max)
                    tt(oh, t1, wide(r4[6]), ALU.is_equal)
                    tt(t1, oh, pb, ALU.mult)
                    red(gates[:, n, :], t1, ALU.add)
                    if n == 0:
                        ts(t1, oh, NEG, None, ALU.mult)
                        tt(t0, t0, t1, ALU.add)
                    tt(oh, oh, wide(valid), ALU.mult)
                tt(mask, oh1, oh2, ALU.add)
                dve.sem_inc(hot_done, 1)
                tt(r4[7], gates[:, 0, :], gates[:, 1, :], ALU.add)
                then(dve.reciprocal(r4[8], r4[7]))
                tt(gates[:, 0, :], gates[:, 0, :], r4[8], ALU.mult)
                tt(gates[:, 1, :], gates[:, 1, :], r4[8], ALU.mult)
                for k, oh in ((0, oh1), (1, oh2)):
                    tt(vals[:, k, :, 0:NE], oh, wide(CT[:, C_ROW:C_ROW + 4]), ALU.mult)
                    tt(vals[:, k, :, NE:2 * NE], oh, wide(CT[:, C_ROW + 4 * k:C_ROW + 4 * k + 4]), ALU.mult)
                dve.wait_ge(rank_ps, l + 1)
                then(dve.tensor_copy(rk, PS[:, 2, 0:64].rearrange("p (t e) -> p t e", t=4)))
                tot = t0
                then(dve.tensor_copy(tot, PS[:, 3, 0:64].rearrange("p (t e) -> p t e", t=4)))
                for j in range(1, 4):
                    tt(rk[:, j:4, :], rk[:, j:4, :], tot[:, j - 1:j, :].broadcast_to([P, 4 - j, NE]), ALU.add)
                tt(t1[:, 0, :], tot[:, 0, :], tot[:, 1, :], ALU.add)
                tt(t1[:, 1, :], tot[:, 2, :], tot[:, 3, :], ALU.add)
                tt(t1[:, 2, :], t1[:, 0, :], t1[:, 1, :], ALU.add)
                red(r4[9][:, 0:1], t1[:, 2, :], ALU.max)
                ts(r4[9][:, 1:2], r4[9][:, 0:1], float(P), None, ALU.is_gt)
                ts(r4[9][:, 2:3], r4[9][:, 0:1], float(2 * P), None, ALU.is_gt)
                ts(r4[9][:, 3:4], r4[9][:, 0:1], float(3 * P), None, ALU.is_gt)
                red(r4[10][:, 0:1], r4[9][:, 1:4], ALU.add)
                dve.tensor_copy(more_rounds[:, :], r4[10][0:1, 0:1]).then_inc(routed, 1)
                for k, oh in ((0, oh1), (1, oh2)):
                    tt(t1, oh, rk, ALU.mult)
                    red(r4[k], t1, ALU.add)

            def moe_round(l, rb, r):
                for k in range(2):
                    last = dve.tensor_tensor(hot[k], CT[:, C_IOTA:C_IOTA + P].unsqueeze(1).broadcast_to([P, 4, P]),
                                             r4[k].unsqueeze(2).broadcast_to([P, 4, P]), ALU.is_equal)
                last.then_inc(idx_in, 1)
                dve.wait_ge(idx_ps, rb + r + 1)
                dve.tensor_scalar(idx[:, :, :], PS[:, 7, 0:2 * NE].rearrange("p (k e) -> p k e", k=2), FAR, None,
                                  ALU.add).then_inc(idx_ready, 1)

                def turned(i, par):
                    E = 16 * (rb + r) + 2 * i + par
                    dve.wait_ge(xt_ps, 2 * E + 1)
                    dve.tensor_copy(xgT[par][:, 0:4, :].rearrange("p k s -> p (k s)"), PS[:, 2, :]
                                    ).then_inc(xt_dve, 1)

                def result(i, par, first):
                    E = 16 * (rb + r) + 2 * i + par
                    dve.wait_ge(o_ps, 2 * E + 1)
                    if not first:
                        dve.wait_ge(scat[par], 16 * (PAIRS * (rb + r) + i))
                    dve.tensor_copy(ob[par][:, 0:512], PS[:, 5, :]).then_inc(o_dve, 1)

                def gated(i, par):
                    E = 16 * (rb + r) + 2 * i + par
                    dve.wait_ge(silu_done, E + 1)
                    dve.wait_ge(up_ps, E + 1)
                    dve.tensor_tensor(hid, hid, PS[:, 1, :], ALU.mult).then_inc(hid_done, 1)

                def pair(i, first, last):
                    gated(i, 0)
                    turned(i, 1)
                    if not first:
                        result(i - 1, 1, isinstance(i, int) and i == 1)
                    gated(i, 1)
                    if not last:
                        turned(i + 1, 0)
                    result(i, 0, first)

                turned(0, 0)
                pair(0, True, False)
                pair(1, False, False)
                with dve.Fori(2, PAIRS - 1) as i:
                    pair(i, False, False)
                pair(PAIRS - 1, False, True)
                result(PAIRS - 1, 1, False)
                dve.wait_ge(round_closed, rb + r + 1)
                for k in range(2):
                    last = dve.tensor_scalar(r4[k], r4[k], float(P), None, ALU.subtract)
                    last.then_inc(rank_moved, 1)
                dve.wait_ge(rank_moved, 2 * (rb + r) + 2)

            w_read = {}
            then(dve.memset(lam[:, 6:7], EPS))
            then(dve.memset(qz[:, :, :, :, :].rearrange("p h b m t -> p (h b m t)"), 0.0))
            dve.wait_ge(x_in, 64)
            for j in range(4):
                ln_front(0, j)
            for j in range(4):
                ln_back(0, j)
            dve.wait_ge(cols_in, 16 * (2 + 8 + 1))
            l4 = lq.rearrange("p l (i d) -> p l i d", i=4)
            for l in range(DEPTH):
                then(dve.tensor_tensor(l4[:, l, 0:4:2, :], l4[:, l, 0:4:2, :], l4[:, l, 1:4:2, :], ALU.mult))
                last = dve.tensor_reduce(lam[:, 2 + 2 * l:4 + 2 * l], l4[:, l, 0:4:2, :], X, ALU.add)
                last.then_inc(lam_sum, 1)
            dve.wait_ge(lam_exp, 1)
            for l in range(DEPTH):
                then(dve.tensor_tensor(lam[:, l:l + 1], lam[:, 3 + 2 * l:4 + 2 * l], lam[:, 2 + 2 * l:3 + 2 * l],
                                       ALU.subtract))
                then(dve.tensor_scalar(lam[:, l:l + 1], lam[:, l:l + 1], -LAM_INIT[l], None, ALU.add))
                then(dve.tensor_scalar(cols[:, l:l + 1], cols[:, l:l + 1], 1.0 - LAM_INIT[l], None, ALU.mult))
            dve.sem_inc(lam_done, 1)
            turn_h(0)
            rb = 0
            for l in range(DEPTH):
                dve.wait_ge(proj_sb, 16 * l + 4)
                for m in range(2):
                    last = dve.tensor_copy(qz[64 * m:64 * m + 64, :, :, m, :],
                                           qT[64 * m:64 * m + 64, :, DEC:NTOK].rearrange("p h (b t) -> p h b t", b=DB))
                last.then_inc(qz_done, 1)
                for j in range(STEPS):
                    if j < 8:
                        task(l, "cachek", j)
                        task(l, "past", j)
                    if j < len(UNITS):
                        front(l, j)
                    if j >= 2:
                        task(l, "w", j - 2)
                    if 1 <= j <= len(UNITS):
                        back(l, j - 1)
                for h in range(HEADS):
                    rs = pr[h % 2].rearrange("p m n -> p (m n)")[:, 0:NTOK]
                    dve.wait_ge(rms_done, 4 * l + h + 1)
                    then(dve.reciprocal(rs, rs))
                    dve.scalar_tensor_tensor(FT[:, h, :], OT[:, h, :], cols[:, l:l + 1], rs, ALU.mult,
                                             ALU.mult).then_inc(mix_done, 1)
                q = LN1[l]
                for j in range(4):
                    n = TN[j]
                    dve.wait_ge(op_ps, 4 * l + j + 1)
                    b = 6 * (j % 2)
                    c = did(dve.scalar_tensor_tensor(H[0:n, j, :], H[0:n, j, :], ALPHA,
                                                     PS[0:n, b:b + 2, :].rearrange("p k n -> p (k n)"), ALU.mult,
                                                     ALU.add))
                    after(c)
                    dve.sem_inc(res_done, 1)
                    ln_front(q, j)
                    ln_back(q, j)
                turn_h(q)
                route(l)
                more = dve.value_load(more_rounds[0:1, 0:1], min_val=0, max_val=3)
                R = more + 1
                with dve.Fori(0, R) as r:
                    moe_round(l, rb, r)
                rb = rb + R
                q = LN2[l]
                for j in range(4):
                    n = TN[j]
                    y = yb[j % 2][0:n]
                    dve.wait_ge(y_in[j % 2], 16 * (2 * l + j // 2 + 1))
                    then(dve.tensor_scalar(y[:, 0, :], y[:, 0, :], gates[0:n, 0, j:j + 1], None, ALU.mult))
                    then(dve.scalar_tensor_tensor(y[:, 0, :], y[:, 1, :], gates[0:n, 1, j:j + 1], y[:, 0, :], ALU.mult,
                                                  ALU.add))
                    c = did(dve.scalar_tensor_tensor(H[0:n, j, :], H[0:n, j, :], ALPHA, y[:, 0, :], ALU.mult, ALU.add))
                    after(c)
                    dve.sem_inc(comb, 1)
                    ln_front(q, j)
                    if j >= 1:
                        ln_back(q, j - 1)
                ln_back(q, 3)
                if l + 1 < DEPTH:
                    turn_h(q)

        @block.scalar
        def _(act):
            def load_gb(q, g, b):
                for k, row in ((0, g), (1, b)):
                    act.dma_start(gb[:, k, :], row.partition_broadcast(P)).then_inc(gb_in, 16)

            def load_ckv(l, n):
                if n >= 8:
                    if n < 12:
                        act.wait_ge(task_ps, l * N_TASK + TASK["cachek", n - 4] + 1)
                    else:
                        act.wait_ge(cv_used, 8 * l + n - 11)
                elif n >= 4:
                    act.wait_ge(task_ps, l * N_TASK + TASK["cachek", n - 4] + 1)
                src = t["cache_k"] if n < 8 else t["cache_v"]
                act.dma_start(ckv[n % 4], src[l, n % 8].rearrange("s h e -> s (h e)")).then_inc(ckv_in[n % 4], 16)

            def turn_h(q):
                for j in range(4):
                    bank = 3 + 2 * (j % 2)
                    act.wait_ge(hx_ps, 8 * q + 2 * j + 2)
                    act.activation(FT[:, 4:8, TC[j]:TC[j] + TN[j]],
                                   PS[:, bank, :].rearrange("p (k n) -> p k n", k=4)[:, :, 0:TN[j]],
                                   ACT.Copy).then_inc(hx_act, 1)

            def proj(l, m):
                act.wait_ge(proj_ps, 16 * l + m + 1)
                if m < 4:
                    dst = qT[:, m, :]
                elif m < 8:
                    dst = kT[:, m - 4, :]
                elif m < 12:
                    dst = vT
                    if m > 8:
                        act.wait_ge(task_ps, l * N_TASK + TASK["vu", m - 9] + 1)
                else:
                    dst = D4[:, m - 12, :]
                act.activation(dst, PS[:, m % 2, 0:NTOK], ACT.Copy).then_inc(proj_sb, 1)

            def task(l, kind, n):
                i = TASK[kind, n]
                bank = 4 + i % 2
                act.wait_ge(task_ps, l * N_TASK + i + 1)
                done = emptied(l, i)[1]
                if kind == "state":
                    act.activation(stT, PS[:, bank, 0:480].rearrange("p (g n) -> p g n", g=4),
                                   ACT.Copy).then_inc(task_act, 1)
                elif kind == "k" or n < 4:
                    dst = kout if kind == "k" else V[:, :, n * P:(n + 1) * P]
                    if kind == "k" and (n > 0):
                        act.wait_ge(k_out, 48 * (4 * l + n))
                    act.activation(dst[:, 0:3, :], PS[:, bank, 0:384].rearrange("p (t e) -> p t e", t=3), ACT.Copy)
                    act.activation(dst[0:NMETA, 3, :], PS[0:NMETA, bank, 384:512], ACT.Copy).then_inc(task_act, 1)
                    if kind == "k":
                        act.wait_ge(task_act, done)
                        act.dma_start(o["new_k_prompt"][l, 0, NMETA:, n, :].rearrange("(t p) e -> p t e", p=P),
                                      kout[:, 0:2, :]).then_inc(k_out, 16)
                        act.dma_start(o["new_k_sample"][l, :, :, n, :].rearrange("b t e -> (b t) e"),
                                      kout[:, 2, :]).then_inc(k_out, 16)
                        act.dma_start(o["new_k_prompt"][l, 0, 0:NMETA, n, :], kout[0:NMETA, 3, :]).then_inc(k_out, 16)
                    elif n == 3:
                        act.wait_ge(task_act, done)
                        act.dma_start(o["new_v_prompt"][l, 0, NMETA:].rearrange("(t p) h e -> p t (h e)", p=P),
                                      V[:, 0:2, :]).then_inc(v_out, 16)
                        act.dma_start(o["new_v_sample"][l].rearrange("b t h e -> (b t) (h e)"),
                                      V[:, 2, :]).then_inc(v_out, 16)
                        act.dma_start(o["new_v_prompt"][l, 0, 0:NMETA].rearrange("t h e -> t (h e)"),
                                      V[0:NMETA, 3, :]).then_inc(v_out, 16)
                else:
                    g = n - 4
                    if g > 0:
                        act.wait_ge(u_out, 32 * (4 * l + g))
                    act.activation(uout, PS[:, bank, 0:256].rearrange("p (t e) -> p t e", t=2),
                                   ACT.Copy).then_inc(task_act, 1)
                    act.wait_ge(task_act, done)
                    act.dma_start(o["new_pool_prompt"][l, 0, :, g * P:(g + 1) * P],
                                  uout[P - STATE:P, 0, :]).then_inc(u_out, 16)
                    act.dma_start(us[l, :, :, g * P:(g + 1) * P].rearrange("b t e -> (b t) e"),
                                  uout[:, 1, :]).then_inc(u_out, 16)

            def exps(l, i):
                kind, h = UNITS[i]
                x = pr[i % 2]
                act.wait_ge(score_max, 13 * l + i + 1)
                if kind == "meta":
                    xm = x[0:NMETA].rearrange("p m n -> p (m n)")[:, 0:128]
                    act.activation(xm, xm, ACT.Exp, scale=SCALE).then_inc(exp_done, 1)
                    return
                n = {"frames1": 272, "frames0": 144, "decode": 256}[kind]
                sm = small[:, 12 * (i % 4):12 * (i % 4) + 12]
                for m in range(2):
                    last = act.activation(x[:, m, 0:n], x[:, m, 0:n], ACT.Exp, bias=sm[:, 2 + m:3 + m], scale=SCALE,
                                          accum_out=sm[:, 4 + m:5 + m])
                last.then_inc(exp_done, 1)

            def heads_out(l, i):
                kind, h = UNITS[i]
                n = i if i < 8 else 8
                if kind == "decode":
                    return
                act.wait_ge(av_ps, 9 * l + n + 1)
                if kind == "meta":
                    act.activation(OT[:, :, 0:NMETA], PS[:, 1, 0:64].rearrange("p (h q) -> p h q", h=HEADS),
                                   ACT.Copy).then_inc(ot_sb, 1)
                else:
                    c = TC[1] if kind == "frames1" else TC[0]
                    act.activation(OT[:, h, c:c + P], PS[:, 6 + i % 2, 0:P], ACT.Copy).then_inc(ot_sb, 1)

            def moe_round(l, rb, r):
                def turned(i, par):
                    E = 16 * (rb + r) + 2 * i + par
                    act.wait_ge(xt_ps, 2 * E + 2)
                    act.activation(xgT[par][:, 4:8, :].rearrange("p k s -> p (k s)"), PS[:, 3, :],
                                   ACT.Copy).then_inc(xt_act, 1)

                def silu(i, par):
                    E = 16 * (rb + r) + 2 * i + par
                    act.wait_ge(gate_ps, E + 1)
                    act.activation(hid, PS[:, 0, :], ACT.Silu).then_inc(silu_done, 1)

                def hid_turned(i, par):
                    E = 16 * (rb + r) + 2 * i + par
                    act.wait_ge(ht_ps, E + 1)
                    act.activation(hidT.rearrange("p k s -> p (k s)"), PS[:, 4, :], ACT.Copy).then_inc(ht_sb, 1)

                def result(i, par, first):
                    E = 16 * (rb + r) + 2 * i + par
                    act.wait_ge(o_ps, 2 * E + 2)
                    if not first:
                        act.wait_ge(scat[par], 16 * (PAIRS * (rb + r) + i))
                    act.activation(ob[par][:, 512:1024], PS[:, 6, :], ACT.Copy).then_inc(o_act, 1)

                def pair(i, first, last):
                    silu(i, 0)
                    turned(i, 1)
                    if not first:
                        result(i - 1, 1, isinstance(i, int) and i == 1)
                    hid_turned(i, 0)
                    silu(i, 1)
                    if not last:
                        turned(i + 1, 0)
                    result(i, 0, first)
                    hid_turned(i, 1)

                turned(0, 0)
                pair(0, True, False)
                pair(1, False, False)
                with act.Fori(2, PAIRS - 1) as i:
                    pair(i, False, False)
                pair(PAIRS - 1, False, True)
                result(PAIRS - 1, 1, False)

            act.dma_start(H[:, 0:2, :], t["x_prompt"][0].rearrange("(t p) n -> p t n", p=P)).then_inc(x_in, 16)
            act.dma_start(H[:, 2, :], t["x_sample"].rearrange("b t n -> (b t) n")).then_inc(x_in, 16)
            act.dma_start(H[0:NMETA, 3, :], t["meta_tokens"]).then_inc(x_in, 16)
            act.dma_start(rb_[:, :], t["router_b"].partition_broadcast(P)).then_inc(x_in, 16)
            load_gb(0, t["ln_in_g"], t["ln_in_b"])
            act.dma_start(CT[:, :], t["consts"]).then_inc(consts_in, 16)
            for l in range(DEPTH):
                act.dma_start(cols[:, l:l + 1], t["subln_w"][l].rearrange("(p o) -> p o", o=1)).then_inc(cols_in, 16)
                for g in range(4):
                    act.dma_start(cols[:, 2 + 4 * l + g:3 + 4 * l + g],
                                  t["pool_scale"][l, g * P:(g + 1) * P].rearrange("(p o) -> p o", o=1)
                                  ).then_inc(cols_in, 16)
            act.dma_start(lq.rearrange("p l n -> p (l n)"),
                          t["lambda_qk"].rearrange("l i d -> (l i d)").partition_broadcast(P)).then_inc(cols_in, 16)
            act.dma_start(rw[:, :, :], t["router_w"].rearrange("(k p) e -> p k e", p=P)).then_inc(consts_in, 16)
            act.wait_ge(lam_sum, DEPTH)
            act.activation(lam[:, 2:6], lam[:, 2:6], ACT.Exp).then_inc(lam_exp, 1)
            turn_h(0)
            rb = 0
            for l in range(DEPTH):
                if l == 0:
                    act.wait_ge(lam_done, 1)
                act.dma_start(spin[0:120, :], t["state_pool"][l].rearrange("b s n -> (b s) n")).then_inc(state_in, 16)
                for n in range(4):
                    load_ckv(l, n)
                act.dma_start(wpool[:, :, :], t["w_pool"][l].rearrange("g c e -> c g e")).then_inc(wpool_in, 16)
                for m in range(8):
                    proj(l, m)
                task(l, "state", 0)
                for j in range(STEPS):
                    if j < 8:
                        load_ckv(l, 4 + j)
                        proj(l, 8 + j)
                        if j < 4:
                            task(l, "k", j)
                    if 1 <= j <= 8:
                        task(l, "vu", j - 1)
                    if j < len(UNITS):
                        exps(l, j)
                    if j >= 2:
                        heads_out(l, j - 2)
                for g in range(4):
                    act.wait_ge(pm_ps, 4 * l + g + 1)
                    act.activation(FT[:, 4 + g, :], PS[:, 6 + g % 2, 0:NTOK], ACT.Copy,
                                   scale=cols[:, 2 + 4 * l + g:3 + 4 * l + g]).then_inc(pm_sb, 1)
                for n in range(12, 16):
                    load_ckv(l, n)
                act.wait_ge(cv_used, 8 * (l + 1))
                act.activation(OT[:, :, DEC:NTOK], PS[:, 0, :].rearrange("p (h q) -> p h q", h=HEADS),
                               ACT.Copy).then_inc(ot_sb, 1)
                act.wait_ge(ot_sb, 10 * (l + 1))
                for h in range(HEADS):
                    act.activation(FT[:, h, :], OT[:, h, :], ACT.Square).then_inc(sq_done, 1)
                for h in range(HEADS):
                    act.wait_ge(ss_ps, 4 * l + h + 1)
                    if h >= 2:
                        act.wait_ge(mix_done, 4 * l + h - 1)
                    act.activation(pr[h % 2].rearrange("p m n -> p (m n)")[:, 0:NTOK], PS[:, 2 + h, 0:NTOK], ACT.Sqrt,
                                   bias=lam[:, 6:7], scale=1.0 / P).then_inc(rms_done, 1)
                act.wait_ge(u_out, 128 * (l + 1))
                act.dma_start(o["new_pool_sample"][l], us[l, :, 1:DS, :]).then_inc(us_out, 16)
                act.wait_ge(mix_done, 4 * (l + 1))
                act.wait_ge(v_out, 48 * (l + 1))
                load_gb(LN1[l], t["ln1_g"][l], t["ln1_b"][l])
                turn_h(LN1[l])
                act.wait_ge(lg_shifted, l + 1)
                act.activation(RT[0].rearrange("p t e -> p (t e)"), RT[0].rearrange("p t e -> p (t e)"),
                               ACT.Exp).then_inc(act_step, 1)
                act.wait_ge(routed, l + 1)
                more = act.value_load(more_rounds[0:1, 0:1], min_val=0, max_val=3)
                R = more + 1
                with act.Fori(0, R) as r:
                    moe_round(l, rb, r)
                rb = rb + R
                act.wait_ge(round_closed, rb)
                for j in range(4):
                    if j >= 2:
                        act.wait_ge(comb, 4 * l + j - 1)
                    act.dma_start(yb[j % 2][0:TN[j]],
                                  ys.rearrange("(k r) n -> k r n", k=2)[:, P * j:P * j + TN[j], :]
                                  .rearrange("k r n -> r k n")).then_inc(y_in[j % 2], 16)
                    if j == 1:
                        load_gb(LN2[l], t["ln2_g"][l], t["ln2_b"][l])
                if l + 1 < DEPTH:
                    turn_h(LN2[l])
                    act.wait_ge(comb, 4 * (l + 1))
            act.wait_ge(k_out, 48 * 4 * DEPTH)
            act.wait_ge(v_out, 48 * DEPTH)
            act.wait_ge(u_out, 128 * DEPTH)
            act.wait_ge(us_out, 16 * DEPTH)

        @block.gpsimd
        def _(pool):
            steps = [0]

            def then(ins):
                steps[0] += 1
                ins.then_inc(pool_step, 1)
                pool.wait_ge(pool_step, steps[0])

            half = CT[:, C_HALF:C_HALF + 1]

            def ln_power(q, j):
                n = TN[j]
                pool.wait_ge(ln_var, 4 * q + j + 1)
                pool.tensor_tensor(stats[0:n, j, 15:16], stats[0:n, j, 14:15], half[0:n, 0:1], ALU.pow
                                   ).then_inc(ln_rstd, 1)

            def ln_bias(q, j):
                n = TN[j]
                pool.wait_ge(ln_scaled, 4 * q + j + 1)
                pool.tensor_tensor(H[0:n, j, :], H[0:n, j, :], gb[0:n, 1, :], ALU.add).then_inc(ln_out, 1)

            def pooling(l, g):
                w = WINDOWS[g]
                pool.wait_ge(proj_sb, 16 * l + 13 + g)
                dec = ue[:, EXT:EW].rearrange("p (b n) -> p b n", b=DB)
                if 4 * l + g > 0:
                    pool.wait_ge(d4_done, 4 * l + g)
                pool.memset(ue[:, 0:STATE], 0.0)
                pool.tensor_copy(ue[:, STATE:EXT], D4[:, g, 0:NMETA + SEQ])
                if g == 0:
                    pool.wait_ge(task_act, emptied(l, TASK["state", 0])[1])
                pool.tensor_copy(dec[:, :, 0:STATE], stT[:, g, :].rearrange("p (b n) -> p b n", b=DB))
                then(pool.tensor_copy(dec[:, :, STATE:STATE + DS],
                                      D4[:, g, DEC:NTOK].rearrange("p (b n) -> p b n", b=DB)))
                src, s, lo = ue, 1, 0
                for n in range(g + 1):
                    dst = (wa, wb)[n % 2]
                    lo += s
                    then(pool.tensor_tensor(dst[:, lo:EW], src[:, lo:EW], src[:, lo - s:EW - s], ALU.add))
                    src, s = dst, 2 * s
                win = src
                then(pool.tensor_tensor(win[:, STATE:STATE + NMETA], win[:, STATE:STATE + NMETA],
                                        CT[:, C_POOL + NMETA * g:C_POOL + NMETA * (g + 1)], ALU.mult))
                then(pool.tensor_scalar(win[:, STATE:EW], win[:, STATE:EW], 1.0 / w, 0.0, ALU.mult, ALU.add))
                pool.wait_ge(task_ps, l * N_TASK + TASK["vu", 4 + g] + 1)
                then(pool.tensor_tensor(D4[:, g, 0:NMETA + SEQ], win[:, STATE:EXT], ue[:, STATE:EXT], ALU.subtract))
                pool.tensor_tensor(D4[:, g, DEC:NTOK].rearrange("p (b n) -> p b n", b=DB),
                                   win[:, EXT:EW].rearrange("p (b n) -> p b n", b=DB)[:, :, STATE:STATE + DS],
                                   dec[:, :, STATE:STATE + DS], ALU.subtract).then_inc(d4_done, 1)

            last_row, last_result = pool.to_reg(NTOK - 1), pool.to_reg(2 * NTOK - 1)

            def gather(e):
                pool.indirect_dma_start(xg[e % 2], None, xs, bass.IndirectOffsetOnAxis(ap=idx[:, 0, e:e + 1], axis=0),
                                        bounds_check=last_row, oob_is_err=False).then_inc(xg_in[e % 2], 16)

            def moe_round(l, rb, r):
                E0 = 16 * (rb + r)
                pool.wait_ge(idx_ready, rb + r + 1)
                pool.sem_inc(pool_past_wait, 1)
                gather(0)
                gather(1)
                for e in range(NE):
                    if e + 2 < NE:
                        pool.wait_ge(xt_ps, 2 * (E0 + e) + 2)
                        pool.sem_inc(pool_past_wait, 1)
                        gather(e + 2)
                    pool.wait_ge(o_dve, E0 + e + 1)
                    pool.wait_ge(o_act, E0 + e + 1)
                    pool.sem_inc(pool_past_wait, 1)
                    pool.indirect_dma_start(ys, bass.IndirectOffsetOnAxis(ap=idx[:, 1, e:e + 1], axis=0), ob[e % 2],
                                            None, bounds_check=last_result, oob_is_err=False
                                            ).then_inc(scat[e % 2], 16)
                for par in range(2):
                    pool.wait_ge(scat[par], 16 * PAIRS * (rb + r + 1))
                pool.sem_inc(round_closed, 1)

            pool.wait_ge(consts_in, 32)
            for j in range(4):
                ln_power(0, j)
            pool.wait_ge(gb_in, 32)
            for j in range(4):
                ln_bias(0, j)
            rb = 0
            for l in range(DEPTH):
                for g in range(4):
                    pooling(l, g)
                for j in range(4):
                    ln_power(LN1[l], j)
                    ln_bias(LN1[l], j)
                    pool.wait_ge(ln_out, 4 * LN1[l] + j + 1)
                    if j == 3:
                        pool.memset(M[:, 0:2048], 0.0).then_inc(xg_zero, 1)
                    pool.dma_start(xs[P * j:P * j + TN[j], :], H[0:TN[j], j, :]).then_inc(xs_out, 16)
                pool.wait_ge(xg_zero, l + 1)
                pool.wait_ge(xs_out, 64 * (l + 1))
                pool.wait_ge(routed, l + 1)
                more = pool.value_load(more_rounds[0:1, 0:1], min_val=0, max_val=3)
                R = more + 1
                with pool.Fori(0, R) as r:
                    moe_round(l, rb, r)
                rb = rb + R
                q = LN2[l]
                ln_power(q, 0)
                for j in range(4):
                    if j < 3:
                        ln_power(q, j + 1)
                    ln_bias(q, j)
            pool.wait_ge(ln_out, 4 * LN2[-1] + 4)
            pool.dma_start(o["y_prompt"][0].rearrange("(t p) n -> p t n", p=P), H[:, 0:2, :]).then_inc(y_out, 16)
            pool.dma_start(o["y_sample"].rearrange("b t n -> (b t) n"), H[:, 2, :]).then_inc(y_out, 16)
            pool.wait_ge(y_out, 32)



_INS = ["x_prompt", "x_sample", "cache_k", "cache_v", "state_pool", "meta_tokens", "ln_in_g", "ln_in_b", "w_in",
        "lambda_qk", "subln_w", "w_pool", "pool_scale", "w_out", "ln1_g", "ln1_b", "router_w", "router_b", "w_gate",
        "w_up", "w_down", "ln2_g", "ln2_b"]
_OUTS = [("y_prompt", (1, SEQ, D)), ("y_sample", (DB, DS, D)),
         ("new_k_prompt", (DEPTH, 1, NMETA + SEQ, HEADS, 2 * HD)), ("new_v_prompt", (DEPTH, 1, NMETA + SEQ, HEADS, 2 * HD)),
         ("new_pool_prompt", (DEPTH, 1, STATE, AW)),
         ("new_k_sample", (DEPTH, DB, DS, HEADS, 2 * HD)), ("new_v_sample", (DEPTH, DB, DS, HEADS, 2 * HD)),
         ("new_pool_sample", (DEPTH, DB, STATE, AW))]


def kernel(**inputs):
    import concourse.bacc as _bacc
    from concourse.bass_utils import run_bass_kernel_spmd as _run

    nc = _bacc.Bacc("TRN2", target_bir_lowering=False, num_devices=1)
    arrays, t, o = {}, {}, {}
    for name in _INS:
        arrays[f"in_{name}"] = np.ascontiguousarray(inputs[name])
    arrays["in_consts"] = const_table()
    for name in _INS + ["consts"]:
        a = arrays[f"in_{name}"]
        t[name] = nc.dram_tensor(f"in_{name}", a.shape, mybir.dt.from_np(a.dtype), kind="ExternalInput").ap()
    for name, shape in _OUTS:
        o[name] = nc.dram_tensor(f"out_{name}", shape, F32, kind="ExternalOutput").ap()
    program(nc, t, o)
    r = _run(nc, [arrays], core_ids=[0])
    return tuple(r.results[0][f"out_{name}"] for name, _ in _OUTS)
```

```python
from contextlib import ExitStack

import numpy as np
import concourse.bass as bass
from concourse import mybir

F32 = mybir.dt.float32
F32R = mybir.dt.float32r
I32 = mybir.dt.int32
U32 = mybir.dt.uint32
ALU = mybir.AluOpType
ACT = mybir.ActivationFunctionType
X = mybir.AxisListType.X

DEPTH, D, NMETA, SEQ, DB, DS, PAST = 2, 1024, 16, 256, 8, 16, 128
P = 128
KT = D // P
HEADS, HD = 4, 64
AW = HEADS * 2 * HD
NTOK = NMETA + SEQ + DB * DS
TC = [16, 144, 272, 0]
TN = [128, 128, 128, 16]
DEC = TC[2]
NE, NG, EPG = 16, 4, 4
DE = 512
ALPHA = float((2 * DEPTH) ** 0.25)
EPS = 1e-5
STATE = 15
WINDOWS = (2, 4, 8, 16)
SLOTS = 6
CH = 4096
SCALE = HD ** -0.5
NEG = -1e30
FAR = 4096.0
PAIRS = NE // 2
SUB = CH // 4
LAM_INIT = [0.8 - 0.6 * float(np.exp(-0.3 * l)) for l in range(DEPTH)]
SLOPES = [2.0 ** (-8.0 * h / HEADS) for h in range(1, HEADS + 1)]

C_ID, C_TRI, C_ONE, C_D1, C_D0, C_DD, C_DM = 0, 128, 256, 384, 656, 800, 1056
C_IOTA, C_PG, C_PE, C_ROW, C_POOL, C_VALID, C_HALF, C_LAST, C_END = 1184, 1312, 1316, 1332, 1340, 1404, 1408, 1410, 1414


def const_table():
    c = np.zeros((P, C_END), np.float32)
    i = np.arange(P)
    c[:, C_ID:C_ID + P] = np.eye(P)
    c[:, C_TRI:C_TRI + P] = i[:, None] < i[None, :]
    c[:, C_ONE:C_ONE + P] = 1.0
    kpos = np.arange(NMETA + SEQ)
    kch = np.where(kpos < NMETA, -1, (kpos - NMETA) // 64)

    def dist(qp, kp, seen):
        return np.where(seen, -np.abs(qp[:, None] - kp[None, :]), NEG).astype(np.float32)

    for col, first, n in ((C_D1, 128, 272), (C_D0, 0, 144)):
        qpos = NMETA + first + i
        c[:, col:col + n] = dist(qpos, kpos[:n], kch[None, :n] <= ((qpos - NMETA) // 64)[:, None])
    b, t = i // DS, i % DS
    c[:, C_DD:C_DD + P] = dist(PAST + t, np.arange(P), np.ones((P, P), bool))
    c[:, C_DD + P:C_DD + 2 * P] = dist(PAST + t, PAST + t, b[:, None] == b[None, :])
    m = np.arange(NMETA)
    for h in range(HEADS):
        for k in range(2):
            o = C_DM + (HEADS * k + h) * NMETA
            c[:NMETA, o:o + NMETA] = -np.abs(m[:, None] - m[None, :]) * SLOPES[h] / SCALE
    c[:, C_IOTA:C_IOTA + P] = i
    c[:, C_PG:C_PG + NG] = NG - np.arange(NG)
    c[:, C_PE:C_PE + NE] = NE - np.arange(NE)
    for t in range(4):
        c[:, C_ROW + t] = P * t + i - FAR
        c[:, C_ROW + 4 + t] = P * t + i - FAR + NTOK
        c[:, C_VALID + t] = i < TN[t]
        c[:, C_LAST + t] = t < 3
    for g, w in enumerate(WINDOWS):
        c[:, C_POOL + NMETA * g:C_POOL + NMETA * (g + 1)] = w / np.minimum(m + 1, w)
    c[:, C_HALF] = -0.5
    return c


def tiles_of(l):
    return range(4) if l + 1 < DEPTH else range(3)


UNITS = [(kind, h) for h in range(HEADS) for kind in ("frames1", "frames0")]
UNITS += [("decode", h) for h in range(HEADS)] + [("meta", 0)]
STEPS = len(UNITS) + 2
PROJ_AT = (0, 1, 2, 3, 4, 5, 6, 7)
BLOCK_AT = {j: n for n, j in enumerate(PROJ_AT)}


def transposed_tasks():
    out = [("state", 0, "act")]
    for j in range(STEPS):
        if j < 8:
            out += [("cachek", j, "dve"), ("past", j, "dve")]
            if j < 4:
                out.append(("k", j, "act"))
        if j - 1 in BLOCK_AT:
            out.append(("vu", BLOCK_AT[j - 1], "act"))
        if j >= 2:
            out.append(("w", j - 2, "dve"))
    return out


TASKS = transposed_tasks()
TASK = {(kind, n): i for i, (kind, n, _) in enumerate(TASKS)}
N_TASK = len(TASKS)
N_ACT = sum(e == "act" for _, _, e in TASKS)
N_DVE = N_TASK - N_ACT


def emptied(l, i):
    e = TASKS[i][2]
    n = sum(x[2] == e for x in TASKS[:i + 1])
    return e, l * (N_ACT if e == "act" else N_DVE) + n


def program(nc, t, o):
    ctx = ExitStack()
    with ctx:
        start = {}

        def sb(name, shape, dt=F32):
            out = ctx.enter_context(nc.sbuf_tensor(name, shape, dt))
            start[name] = nc.sbuf_base - 4 * int(np.prod(shape[1:]))
            return out

        def rounded(name, base, first, n):
            return nc.alloc_sbuf_tensor_at(name, [P, n], F32R, offset=start[base] + 4 * first)

        def sem(name):
            return ctx.enter_context(nc.semaphore(name))

        PS = ctx.enter_context(nc.psum_tensor("PS", [P, 8, 512], F32))
        ring = sb("ring", [P, SLOTS, CH])
        H = sb("H", [P, 4, D])
        FT = sb("FT", [P, KT, NTOK])
        QK = sb("QK", [P, 2 * HEADS * NTOK])
        CT = sb("CT", [P, C_END - 0])
        M = sb("M", [P, 7216])
        N = sb("N", [P, 5608])
        DD = sb("DD", [P, 4 * NTOK])
        qz = sb("qz", [P, HEADS, DB, 2, DS])
        wpool = sb("wpool", [P, 4, P])
        cols = sb("cols", [P, 16])
        lam = sb("lam", [P, 8])
        stats = sb("stats", [P, 4, 16])
        gates = sb("gates", [P, 2, 4])
        idx = sb("idx", [P, 2, NE], U32)
        more_rounds = sb("more_rounds", [1, 1], I32)

        ident, tri, ones = (CT[:, c:c + P] for c in (C_ID, C_TRI, C_ONE))
        qT, kT = (QK[:, HEADS * NTOK * i:HEADS * NTOK * (i + 1)].rearrange("p (h n) -> p h n", h=HEADS)
                  for i in range(2))
        ckv = [M[:, 512 * i:512 * i + 512] for i in range(4)]
        D4 = DD[:, :].rearrange("p (g n) -> p g n", g=4)
        kout = M[:, 2048:2560].rearrange("p (t e) -> p t e", t=4)
        OT = M[:, 2560:4160].rearrange("p (h n) -> p h n", h=HEADS)
        uout = M[:, 4160:4416].rearrange("p (t e) -> p t e", t=2)
        V = M[:, 4416:6464].rearrange("p (t n) -> p t n", t=4)
        Wt = M[:, 6464:6736]
        stT = M[:, 6736:7216].rearrange("p (g n) -> p g n", g=4)
        pr = [N[:, 544 * i:544 * i + 544].rearrange("p (m n) -> p m n", m=2) for i in range(2)]
        WT = [N[:, 1088 + 384 * i:1472 + 384 * i].rearrange("p (k q) -> p k q", k=3) for i in range(2)]
        ST = N[:, 1856:2880].rearrange("p (h m q) -> p h m q", h=HEADS, m=2)
        kct = N[:, 2880:3392].rearrange("p (h k) -> p h k", h=HEADS)
        WTp = N[:, 3392:3904].rearrange("p (h q) -> p h q", h=HEADS)
        EXT = STATE + NMETA + SEQ
        EW = EXT + DB * (STATE + DS)
        ue, wa, wb = (N[:, 3904 + EW * i:3904 + EW * (i + 1)] for i in range(3))
        spin, vT = wa[:, 0:512], wb[:, 0:NTOK]
        small = N[:, 5512:5608]
        RT = [N[:, 64 * i:64 * i + 64].rearrange("p (t e) -> p t e", t=4) for i in range(14)]
        lgT = N[0:NE, 900:1300]
        hot = [N[:, 1300 + 512 * k:1812 + 512 * k].rearrange("p (t s) -> p t s", t=4) for k in range(2)]
        vals = N[:, 2324:2580].rearrange("p (k t n) -> p k t n", k=2, t=4)
        r4 = [N[:, 2580 + 4 * i:2584 + 4 * i] for i in range(12)]
        pairs6 = N[:, 2640:2736].rearrange("p (t g n) -> p t g n", t=4, g=4)
        g4 = [N[:, 2736 + 16 * i:2752 + 16 * i].rearrange("p (t g) -> p t g", t=4) for i in range(4)]
        rw = sb("rw", [P, KT, NE])
        rb_ = sb("rb_", [P, NE])
        xg = [M[:, 1024 * i:1024 * i + 1024] for i in range(2)]
        x_hi = [rounded(f"x_hi{i}", "M", 2048 + 1024 * i, 1024) for i in range(2)]
        x_lo = [rounded("x_lo0", "N", 3840, 1024), rounded("x_lo1", "DD", 0, 1024)]
        w_hi = [rounded(f"w_hi{i}", "QK", SUB * i, SUB) for i in range(3)] + [rounded("w_hi3", "N", 2816, SUB)]
        w_lo = rounded("w_lo", "ring", 0, SLOTS * CH)
        h_hi, h_lo = rounded("h_hi", "M", 6656, 512), rounded("h_lo", "DD", 1024, 512)
        ob = [M[:, 4096 + 1024 * i:5120 + 1024 * i] for i in range(2)]
        hid = M[:, 6144:6656]
        yb = [a.rearrange("p (k n) -> p k n", k=2) for a in (M[:, 0:2048], M[:, 2048:4096], QK[:, 0:2048],
                                                             N[:, 2816:4864])]
        gb = M[:, 4096:6144].rearrange("p (k n) -> p k n", k=2)
        lq = M[:, 0:512].rearrange("p (l n) -> p l n", l=DEPTH)

        xs = nc.dram_tensor("xs", (NTOK, D), F32, kind="Internal").ap()
        ys = nc.dram_tensor("ys", (2 * NTOK, D), F32, kind="Internal").ap()
        us = nc.dram_tensor("us", (DEPTH, DB, DS, AW), F32, kind="Internal").ap()

        landed = [sem(f"slot_landed{s}") for s in range(SLOTS)]
        x_in, consts_in, cols_in, gb_in = sem("x_in"), sem("consts_in"), sem("cols_in"), sem("gb_in")
        ckv_in = [sem(f"ckv_in{i}") for i in range(4)]
        state_in, wpool_in = sem("state_in"), sem("wpool_in")
        lam_sum, lam_exp, lam_done, qz_zero = sem("lam_sum"), sem("lam_exp"), sem("lam_done"), sem("qz_zero")
        dve_step, pool_step, act_step = sem("dve_step"), sem("pool_step"), sem("act_step")
        ln_var, ln_rstd, ln_scaled, ln_out = sem("ln_var"), sem("ln_rstd"), sem("ln_scaled"), sem("ln_out")
        hx_ps, hx_dve, hx_act = sem("hx_ps"), sem("hx_dve"), sem("hx_act")
        proj_ps, proj_sb, qz_done = sem("proj_ps"), sem("proj_sb"), sem("qz_done")
        task_ps, task_act, task_dve = sem("task_ps"), sem("task_act"), sem("task_dve")
        score_ps, score_max, exp_done, w_done = sem("score_ps"), sem("score_max"), sem("exp_done"), sem("w_done")
        av_ps, ot_sb = sem("av_ps"), sem("ot_sb")
        cv_used = sem("cv_used")
        d4_done, pm_ps, pm_sb = sem("d4_done"), sem("pm_ps"), sem("pm_sb")
        sq_done, ss_ps, rms_done, mix_done = sem("sq_done"), sem("ss_ps"), sem("rms_done"), sem("mix_done")
        k_out, v_out, u_out, us_out = sem("k_out"), sem("v_out"), sem("u_out"), sem("us_out")
        op_ps, res_done = sem("op_ps"), sem("res_done")
        xs_out = sem("xs_out")
        lg_ps, lg_sb, lgt_ps, hot_done, rank_ps, idx_in, idx_ps, idx_ready, routed = (
            sem("lg_ps"), sem("lg_sb"), sem("lgt_ps"), sem("hot_done"), sem("rank_ps"), sem("idx_in"), sem("idx_ps"),
            sem("idx_ready"), sem("routed"))
        xg_in = [sem(f"xg_in{i}") for i in range(2)]
        xg_zero = sem("xg_zero")
        xt_ps, xt_hi, xt_lo = sem("xt_ps"), sem("xt_hi"), sem("xt_lo")
        up_hi, up_lo, up_used = sem("up_hi"), sem("up_lo"), sem("up_used")
        down_hi, down_lo, down_used = sem("down_hi"), sem("down_lo"), sem("down_used")
        silu_done, hid_done = sem("silu_done"), sem("hid_done")
        ht_ps, ht_hi, ht_lo, o_sb = sem("ht_ps"), sem("ht_hi"), sem("ht_lo"), sem("o_sb")
        scat = [sem(f"scattered{i}") for i in range(2)]
        round_closed = sem("round_closed")
        y_scaled = sem("y_scaled")
        y_in = [sem(f"y_in{i}") for i in range(4)]
        comb = sem("combined")
        y_out = sem("y_out")
        lg_shifted, rank_moved = sem("lg_shifted"), sem("rank_moved")
        pool_past_wait = sem("pool_past_wait")

        block = ctx.enter_context(nc.Block())

        def dense_use(l, rb):
            return l + PAIRS * rb

        def round_use(l, rb, r):
            return l + 1 + PAIRS * (rb + r)

        def quarter(s, j):
            c = s * CH + j * SUB
            return ring[:, s, j * SUB:(j + 1) * SUB], w_lo[:, c:c + SUB]

        def ln_tiles(q):
            return tiles_of((q - 1) // 2) if q else range(4)

        def ln_count(q, j):
            return sum(len(ln_tiles(p)) for p in range(q)) + j + 1

        LN1 = [1, 3]
        LN2 = [2, 4]

        @block.sync
        def _(sp):
            def load(s, view):
                n = view.shape[-1]
                sp.dma_start(ring[:, s, :].rearrange("p (k n) -> p k n", n=n), view).then_inc(landed[s], 16)

            def expert(w, l, e):
                return w[l, bass.ds(e, 1), :, :].rearrange("o (k p) n -> p (o k) n", p=P)

            def load_up(l, e, s, E, dense):
                for n, (w, was) in enumerate((("w_gate", dense[0]), ("w_up", dense[1]))):
                    if was is None:
                        sp.wait_ge(up_used, 8 * E - 12 + 4 * n)
                    else:
                        sp.wait_ge(*was)
                    load(s + n, expert(t[w], l, e))

            def load_down(l, e, s, E, was):
                if was is None:
                    sp.wait_ge(down_used, 4 * E - 4)
                else:
                    sp.wait_ge(*was)
                load(s, expert(t["w_down"], l, e))

            def round_(l, E0, first_round):
                d = [(proj_ps, 16 * l + 4), (proj_ps, 16 * l + 8), (proj_ps, 16 * l + 12), (proj_ps, 16 * l + 16),
                     (op_ps, 4 * l + len(tiles_of(l))), (op_ps, 4 * l + len(tiles_of(l)))] if first_round else [None] * SLOTS
                load_up(l, 0, 0, E0, d[0:2])
                load_up(l, 1, 3, E0 + 1, d[3:5])
                load_down(l, 0, 5, E0, d[5])
                load_up(l, 2, 0, E0 + 2, [None] * 2)
                load_down(l, 1, 2, E0 + 1, d[2])
                load_up(l, 3, 3, E0 + 3, [None] * 2)
                load_down(l, 2, 5, E0 + 2, None)
                with sp.Fori(2, PAIRS) as i:
                    e = 2 * i
                    load_up(l, e, 0, E0 + e, [None] * 2)
                    load_down(l, e - 1, 2, E0 + e - 1, None)
                    load_up(l, e + 1, 3, E0 + e + 1, [None] * 2)
                    load_down(l, e, 5, E0 + e, None)
                load_down(l, NE - 1, 2, E0 + NE - 1, None)

            rb = 0
            sp.wait_ge(x_in, 64)
            sp.wait_ge(gb_in, 32)
            for l in range(DEPTH):
                if l > 0:
                    last = [(up_used, 128 * more + 116), (up_used, 128 * more + 120), (down_used, 64 * rb),
                            (up_used, 128 * more + 124), (up_used, 128 * rb), (down_used, 64 * more + 60)]
                for s in (0, 1, 3, 4, 5, 2) if l > 0 else range(SLOTS):
                    w, c = ("w_in", s) if s < 4 else ("w_out", s - 4)
                    if l > 0 and s == 3:
                        for j in range(4):
                            sp.wait_ge(y_in[j], 16 * l)
                    if l > 0:
                        sp.wait_ge(*last[s])
                    load(s, t[w][l, :, c * 512:(c + 1) * 512].rearrange("(k p) n -> p k n", p=P))
                round_(l, 16 * rb, True)
                sp.wait_ge(routed, l + 1)
                more = sp.value_load(more_rounds[0:1, 0:1], min_val=0, max_val=3)
                R = more + 1
                with sp.If(more > 0):
                    with sp.Fori(1, R) as r:
                        round_(l, 16 * (rb + r), False)
                rb = rb + R

        @block.tensor
        def _(pe):
            def chunk(s, use):
                pe.wait_ge(landed[s], 16 * (use + 1))

            def logits(q, tiles, c0, c1):
                for j in tiles:
                    pe.wait_ge(hx_dve, 4 * q + j + 1)
                    pe.wait_ge(hx_act, 4 * q + j + 1)
                for k in range(KT):
                    mm = pe.matmul(PS[0:NE, 0, c0:c1], rw[:, k, :], FT[:, k, c0:c1], start=(k == 0),
                                   stop=(k == KT - 1))
                mm.then_inc(lg_ps, 1)

            def turn_h(q):
                for j in ln_tiles(q):
                    if q == LN1[-1] and j == 2:
                        pe.wait_ge(res_done, 2 * (q + 1) - 1)
                        logits(q, (0, 1), 0, DEC)
                    elif q in LN1 and j == 3:
                        pe.wait_ge(res_done, 2 * (q + 1) - 1)
                        logits(q, (0, 1, 2), NMETA, NTOK)
                    n = 4 * q + j
                    pe.wait_ge(ln_out, n + 1)
                    if n >= 2:
                        pe.wait_ge(hx_dve, n - 1)
                        pe.wait_ge(hx_act, n - 1)
                    for half in range(2):
                        bank = 2 + 2 * (j % 2) + half
                        for k in range(4):
                            mm = pe.transpose(PS[:, bank, k * P:k * P + TN[j]],
                                              H[0:TN[j], j, (4 * half + k) * P:(4 * half + k + 1) * P],
                                              ident[0:TN[j], 0:TN[j]])
                        mm.then_inc(hx_ps, 1)

            def task_bank(l, i):
                if i >= 2:
                    e, n = emptied(l, i - 2)
                    pe.wait_ge(task_act if e == "act" else task_dve, n)
                return 4 + i % 2

            def proj(l, m, use):
                s = m // 4
                if m % 4 == 0:
                    chunk(s, use)
                if m >= 2:
                    pe.wait_ge(proj_sb, 16 * l + m - 1)
                w = ring[:, s, :].rearrange("p (k n) -> p k n", k=KT)
                for k in range(KT):
                    mm = pe.matmul(PS[:, m % 2, 0:NTOK], w[:, k, (m % 4) * P:(m % 4 + 1) * P], FT[:, k, :],
                                   start=(k == 0), stop=(k == KT - 1))
                mm.then_inc(proj_ps, 1)

            def scores(l, i):
                kind, h = UNITS[i]
                if i >= 1:
                    pe.wait_ge(score_max, 13 * l + i)
                for m in range(2):
                    r = slice(64 * m, 64 * m + 64)
                    if kind in ("frames1", "frames0"):
                        q0, n = (TC[1], 272) if kind == "frames1" else (TC[0], 144)
                        mm = pe.matmul(PS[:, 2 + m, 0:n], qT[r, h, q0:q0 + P], kT[r, h, 0:n], start=True, stop=True)
                    elif kind == "decode":
                        pe.transpose(PS[:, 2 + m, 0:P], ST[:, h, m, :], ident)
                        mm = pe.matmul(PS[:, 2 + m, P:2 * P], qT[r, h, DEC:NTOK], kT[r, h, DEC:NTOK],
                                       start=True, stop=True)
                    else:
                        for g in range(HEADS):
                            c = g * NMETA
                            mm = pe.matmul(PS[0:NMETA, 2 + m, c:c + NMETA], qT[r, g, 0:NMETA], kT[r, g, 0:NMETA],
                                           start=True, stop=True)
                mm.then_inc(score_ps, 1)

            def w_blocks(l, i):
                kind, h = UNITS[i]
                n = TASK["w", i]
                bank = task_bank(l, n)
                pe.wait_ge(w_done, 13 * l + i + 1)
                if kind == "frames1" or kind == "frames0":
                    nb = 2 if kind == "frames1" else 1
                    for k in range(nb):
                        pe.transpose(PS[:, bank, k * P:(k + 1) * P], Wt[:, NMETA + k * P:NMETA + (k + 1) * P], ident)
                    mm = pe.transpose(PS[0:NMETA, bank, nb * P:(nb + 1) * P], Wt[:, 0:NMETA], ident)
                elif kind == "decode":
                    for k in range(2):
                        mm = pe.transpose(PS[:, bank, k * P:(k + 1) * P], Wt[:, k * P:(k + 1) * P], ident)
                else:
                    for g in range(HEADS):
                        mm = pe.transpose(PS[0:NMETA, bank, g * NMETA:(g + 1) * NMETA],
                                          Wt[0:NMETA, g * NMETA:(g + 1) * NMETA], ident[0:NMETA, 0:NMETA])
                mm.then_inc(task_ps, 1)

            def av(l, i):
                kind, h = UNITS[i]
                e, n = emptied(l, TASK["w", i])
                pe.wait_ge(task_dve, n)
                wt = WT[i % 2]
                hs = slice(h * P, (h + 1) * P)
                if kind in ("frames1", "frames0"):
                    _, n = emptied(l, TASK["vu", h])
                    pe.wait_ge(task_act, n)
                    if i >= 2:
                        pe.wait_ge(ot_sb, 10 * l + i - 1)
                    nb = 2 if kind == "frames1" else 1
                    out = PS[:, 6 + i % 2, 0:P]
                    for k in range(nb):
                        pe.matmul(out, V[:, k, hs], wt[:, k, :], start=(k == 0), stop=False)
                    mm = pe.matmul(out, V[0:NMETA, 3, hs], wt[0:NMETA, nb, :], start=False, stop=True)
                    mm.then_inc(av_ps, 1)
                elif kind == "decode":
                    if h == 0:
                        pe.wait_ge(proj_sb, 16 * l + 15)
                    pe.matmul(PS[:, 0, hs], V[:, 2, hs], wt[:, 1, :], start=(h == 0), stop=False,
                              skip_group_check=True)
                else:
                    pe.wait_ge(proj_sb, 16 * l + 16)
                    wm = wt[0:NMETA, 0, 0:HEADS * NMETA].rearrange("p (g q) -> p g q", g=HEADS)
                    for g in range(HEADS):
                        mm = pe.matmul(PS[:, 1, g * NMETA:(g + 1) * NMETA], V[0:NMETA, 3, g * P:(g + 1) * P],
                                       wm[:, g, :], start=True, stop=True)
                    mm.then_inc(av_ps, 1)

            def attention(l, use):
                for m in range(8):
                    proj(l, m, use)
                n = TASK["state", 0]
                bank = task_bank(l, n) if n >= 2 else 4
                pe.wait_ge(state_in, 16 * (l + 1))
                for g in range(4):
                    mm = pe.transpose(PS[:, bank, g * 120:(g + 1) * 120], spin[0:120, g * P:(g + 1) * P],
                                      ident[0:120, 0:120])
                mm.then_inc(task_ps, 1)
                pe.wait_ge(proj_sb, 16 * l + 8)
                for j in range(STEPS):
                    if j < 8:
                        bank = task_bank(l, TASK["cachek", j])
                        pe.wait_ge(ckv_in[j % 4], 16 * (4 * l + j // 4 + 1))
                        for h in range(HEADS):
                            mm = pe.transpose(PS[:, bank, h * P:(h + 1) * P], ckv[j % 4][:, h * P:(h + 1) * P], ident)
                        mm.then_inc(task_ps, 1)
                    if j in BLOCK_AT:
                        proj(l, 8 + BLOCK_AT[j], use)
                    if 3 <= j < 8:
                        av(l, j - 3)
                    if j < 8:
                        bank = task_bank(l, TASK["past", j])
                        pe.wait_ge(task_dve, emptied(l, TASK["cachek", j])[1])
                        if j == 0:
                            pe.wait_ge(qz_done, l + 1)
                        for h in range(HEADS):
                            mm = pe.matmul(PS[:, bank, h * 32:(h + 1) * 32], kct[:, h, :],
                                           qz[:, h, j, :, :].rearrange("p m t -> p (m t)"), start=True, stop=True)
                        mm.then_inc(task_ps, 1)
                        if j < 4:
                            bank = task_bank(l, TASK["k", j])
                            for x in range(4):
                                mm = pe.transpose(PS[0:TN[x], bank, x * P:(x + 1) * P],
                                                  kT[:, j, TC[x]:TC[x] + TN[x]], ident)
                            mm.then_inc(task_ps, 1)
                    if j - 1 in BLOCK_AT:
                        n = BLOCK_AT[j - 1]
                        bank = task_bank(l, TASK["vu", n])
                        pe.wait_ge(proj_sb, 16 * l + 9 + n)
                        tiles = range(4) if n < 4 else (1, 2)
                        src = vT if n < 4 else D4[:, n - 4, :]
                        for y, x in enumerate(tiles):
                            mm = pe.transpose(PS[0:TN[x], bank, y * P:(y + 1) * P], src[:, TC[x]:TC[x] + TN[x]],
                                              ident)
                        mm.then_inc(task_ps, 1)
                    if j < len(UNITS):
                        if UNITS[j][0] == "decode":
                            pe.wait_ge(task_dve, emptied(l, TASK["past", 7])[1])
                        scores(l, j)
                    if j >= 8:
                        av(l, j - 3)
                    if j >= 2:
                        w_blocks(l, j - 2)
                av(l, STEPS - 3)
                def cached_values(streams):
                    for b in streams:
                        pe.wait_ge(ckv_in[b % 4], 16 * (4 * l + 2 + b // 4 + 1))
                        for h in range(HEADS):
                            c = h * P + b * DS
                            mm = pe.matmul(PS[:, 0, c:c + DS], ckv[b % 4][:, h * P:(h + 1) * P],
                                           WTp[:, h, b * DS:(b + 1) * DS], start=False, stop=(b == DB - 1 and h == 3),
                                           skip_group_check=True)
                        mm.then_inc(cv_used, 1)

                cached_values(range(4))
                for g in range(4):
                    if g == 0:
                        pe.wait_ge(ot_sb, 10 * l + 8)
                        if l == 0:
                            pe.wait_ge(wpool_in, 16)
                        else:
                            pe.wait_ge(wpool_in, 32)
                    if g >= 2:
                        pe.wait_ge(pm_sb, 4 * l + g - 1)
                    pe.wait_ge(d4_done, 4 * l + g + 1)
                    pe.matmul(PS[:, 6 + g % 2, 0:NTOK], wpool[:, g, :], D4[:, g, :], start=True,
                              stop=True).then_inc(pm_ps, 1)
                cached_values(range(4, DB))
                for h in range(HEADS):
                    pe.wait_ge(sq_done, 4 * l + h + 1)
                    if h == 0:
                        pe.wait_ge(score_max, 13 * l + 13)
                    if h == 2:
                        pe.wait_ge(task_dve, (l + 1) * N_DVE)
                        pe.wait_ge(task_act, (l + 1) * N_ACT)
                    pe.matmul(PS[:, 2 + h, 0:NTOK], ones, FT[:, h, :], start=True, stop=True).then_inc(ss_ps, 1)

            def out_proj(l, use):
                pe.wait_ge(pm_sb, 4 * (l + 1))
                pe.wait_ge(ot_sb, 10 * (l + 1))
                for half in range(2):
                    chunk(4 + half, use)
                w = [ring[:, 4 + half, :].rearrange("p (k n) -> p k n", k=KT) for half in range(2)]
                for j in tiles_of(l):
                    if j >= 2:
                        pe.wait_ge(res_done, 4 * l + j - 1)
                    for ks in ((4, 5, 6, 7), (0,), (1,), (2,), (3,)):
                        if j == 0 and len(ks) == 1:
                            pe.wait_ge(mix_done, 4 * l + ks[0] + 1)
                        for half in range(2):
                            for k in ks:
                                mm = pe.matmul(PS[0:TN[j], 6 * (j % 2) + half, :], FT[:, k, TC[j]:TC[j] + TN[j]],
                                               w[half][:, k, :], start=(k == 4), stop=(k == 3))
                    mm.then_inc(op_ps, 1)

            def route(l):
                if l + 1 < DEPTH:
                    logits(LN1[l], (3,), 0, NMETA)
                else:
                    logits(LN1[l], (2,), DEC, NTOK)
                pe.wait_ge(lg_sb, l + 1)
                for j in range(4):
                    mm = pe.transpose(PS[0:TN[j], 1, j * NE:(j + 1) * NE], lgT[:, TC[j]:TC[j] + TN[j]],
                                      ident[0:NE, 0:NE])
                mm.then_inc(lgt_ps, 1)
                pe.wait_ge(hot_done, l + 1)
                pe.matmul(PS[:, 2, 0:64], tri, RT[13].rearrange("p t e -> p (t e)"), start=True, stop=True)
                pe.matmul(PS[:, 3, 0:64], ones, RT[13].rearrange("p t e -> p (t e)"), start=True,
                          stop=True).then_inc(rank_ps, 1)

            def moe_round(l, rb, r):
                base = round_use(l, rb, r)

                def turn_x(i, par):
                    E = 16 * (rb + r) + 2 * i + par
                    pe.wait_ge(xg_in[par], 16 * (PAIRS * (rb + r) + i + 1))
                    if not (isinstance(i, int) and i == 0 and par == 0):
                        pe.wait_ge(xt_lo, E)
                    for k in range(KT):
                        mm = pe.transpose(PS[:, 2 + k // 4, k % 4 * P:(k % 4 + 1) * P],
                                          xg[par][:, k * P:(k + 1) * P], ident)
                    mm.then_inc(xt_ps, 1)

                def up(i, par, first):
                    E = 16 * (rb + r) + 2 * i + par
                    pe.wait_ge(xt_hi, E + 1)
                    pe.wait_ge(xt_lo, E + 1)
                    if not first:
                        pe.wait_ge(hid_done, E)
                    for n in range(2):
                        for j in range(4):
                            lo = quarter(3 * par + n, j)[1]
                            pe.wait_ge(up_hi, 8 * E + 4 * n + j + 1)
                            for x in (x_hi[par], x_lo[par]):
                                for k in range(2):
                                    c = (2 * j + k) * P
                                    pe.matmul(PS[:, n, :], x[:, c:c + P], w_hi[j][:, k * 512:(k + 1) * 512],
                                              start=(j == 0 and k == 0 and x is x_hi[par]), stop=False)
                            pe.wait_ge(up_lo, 8 * E + 4 * n + j + 1)
                            for k in range(2):
                                c = (2 * j + k) * P
                                mm = pe.matmul(PS[:, n, :], x_hi[par][:, c:c + P], lo[:, k * 512:(k + 1) * 512],
                                               start=False, stop=(j == 3 and k == 1))
                            mm.then_inc(up_used, 1)

                def turn_hid(i, par, first):
                    E = 16 * (rb + r) + 2 * i + par
                    pe.wait_ge(hid_done, E + 1)
                    if not first:
                        pe.wait_ge(ht_lo, E)
                    for k in range(4):
                        mm = pe.transpose(PS[:, 4, k * P:(k + 1) * P], hid[:, k * P:(k + 1) * P], ident)
                    mm.then_inc(ht_ps, 1)

                def down(i, par, first):
                    E = 16 * (rb + r) + 2 * i + par
                    pe.wait_ge(ht_hi, E + 1)
                    pe.wait_ge(ht_lo, E + 1)
                    if not first:
                        pe.wait_ge(o_sb, E)
                    for j in range(4):
                        lo = quarter(5 if par == 0 else 2, j)[1]
                        c = slice(j * P, (j + 1) * P)
                        pe.wait_ge(down_hi, 4 * E + j + 1)
                        for h in (h_hi, h_lo):
                            for half in range(2):
                                pe.matmul(PS[:, 5 + half, :], h[:, c], w_hi[j][:, half * 512:(half + 1) * 512],
                                          start=(j == 0 and h is h_hi), stop=False)
                        pe.wait_ge(down_lo, 4 * E + j + 1)
                        for half in range(2):
                            mm = pe.matmul(PS[:, 5 + half, :], h_hi[:, c], lo[:, half * 512:(half + 1) * 512],
                                           start=False, stop=(j == 3))
                        mm.then_inc(down_used, 1)

                def pair(i, first, last):
                    up(i, 0, first)
                    turn_x(i, 1)
                    if not first:
                        down(i - 1, 1, False)
                    turn_hid(i, 0, first)
                    up(i, 1, False)
                    if not last:
                        turn_x(i + 1, 0)
                    down(i, 0, first)
                    turn_hid(i, 1, False)

                pe.wait_ge(idx_in, rb + r + 1)
                for k in range(2):
                    for j in range(4):
                        mm = pe.matmul(PS[:, 7, 0:2 * NE], hot[k][:, j, :], vals[:, k, j, :],
                                       start=(k == 0 and j == 0), stop=(k == 1 and j == 3))
                mm.then_inc(idx_ps, 1)
                turn_x(0, 0)
                pair(0, True, False)
                with pe.Fori(1, PAIRS - 1) as i:
                    pair(i, False, False)
                pair(PAIRS - 1, False, True)
                down(PAIRS - 1, 1, False)

            pe.wait_ge(consts_in, 16)
            turn_h(0)
            rb = 0
            for l in range(DEPTH):
                if l > 0:
                    turn_h(LN2[l - 1])
                for j in range(4):
                    pe.wait_ge(hx_dve, 4 * LN2[l - 1] + j + 1 if l else j + 1)
                    pe.wait_ge(hx_act, 4 * LN2[l - 1] + j + 1 if l else j + 1)
                use = dense_use(l, rb)
                attention(l, use)
                out_proj(l, use)
                turn_h(LN1[l])
                route(l)
                pe.wait_ge(routed, l + 1)
                more = pe.value_load(more_rounds[0:1, 0:1], min_val=0, max_val=3)
                R = more + 1
                with pe.Fori(0, R) as r:
                    moe_round(l, rb, r)
                rb = rb + R

        @block.vector
        def _(dve):
            steps = [0]

            def did(ins):
                steps[0] += 1
                ins.then_inc(dve_step, 1)
                return steps[0]

            def after(n):
                dve.wait_ge(dve_step, n)

            def then(ins):
                after(did(ins))

            def ln_front(q, j):
                n = TN[j]
                st = stats[0:n, j, :]
                for half in range(2):
                    c = did(dve.bn_stats(st[:, 6 * half:6 * half + 6], H[0:n, j, half * 512:(half + 1) * 512]))
                after(c)
                then(dve.bn_aggr(st[:, 12:14], st[:, 0:12]))
                dve.tensor_scalar(st[:, 14:15], st[:, 13:14], EPS, None, ALU.add).then_inc(ln_var, 1)

            def ln_back(q, j):
                n = TN[j]
                st = stats[0:n, j, :]
                if j == 0:
                    dve.wait_ge(gb_in, 32 * (q + 1))
                dve.wait_ge(ln_rstd, ln_count(q, j))
                then(dve.tensor_scalar(H[0:n, j, :], H[0:n, j, :], st[:, 12:13], st[:, 15:16], ALU.subtract,
                                       ALU.mult))
                dve.tensor_tensor(H[0:n, j, :], H[0:n, j, :], gb[0:n, 0, :], ALU.mult).then_inc(ln_scaled, 1)

            def turn_h(q):
                for j in ln_tiles(q):
                    bank = 2 + 2 * (j % 2)
                    dve.wait_ge(hx_ps, 8 * q + 2 * j + 1)
                    dve.tensor_copy(FT[:, 0:4, TC[j]:TC[j] + TN[j]],
                                    PS[:, bank, :].rearrange("p (k n) -> p k n", k=4)[:, :, 0:TN[j]]
                                    ).then_inc(hx_dve, 1)

            def front(l, i):
                kind, h = UNITS[i]
                x = pr[i % 2]
                dve.wait_ge(score_ps, 13 * l + i + 1)
                if i >= 2:
                    dve.wait_ge(dve_step, w_read[i - 2])
                sm = small[:, 12 * (i % 4):12 * (i % 4) + 12]
                if kind == "meta":
                    xm = x[0:NMETA].rearrange("p m n -> p (m n)")[:, 0:128].rearrange("p (g n) -> p g n", g=8)
                    mx = small[0:NMETA, 48:56]
                    then(dve.tensor_tensor(xm.rearrange("p (m h) n -> p m (h n)", m=2), PS[0:NMETA, 2:4, 0:64],
                                           CT[0:NMETA, C_DM:C_DM + 128].rearrange("p (m n) -> p m n", m=2), ALU.add))
                    then(dve.tensor_reduce(mx, xm, X, ALU.max))
                    dve.tensor_tensor(xm, xm, mx.unsqueeze(2).broadcast_to([NMETA, 8, NMETA]),
                                      ALU.subtract).then_inc(score_max, 1)
                    return
                col, n = {"frames1": (C_D1, 272), "frames0": (C_D0, 144), "decode": (C_DD, 256)}[kind]
                then(dve.scalar_tensor_tensor(x[:, :, 0:n], CT[:, col:col + n].unsqueeze(1).broadcast_to([P, 2, n]),
                                              SLOPES[h] / SCALE, PS[:, 2:4, 0:n], ALU.mult, ALU.add))
                then(dve.tensor_reduce(sm[:, 0:2], x[:, :, 0:n], X, ALU.max))
                dve.tensor_scalar(sm[:, 2:4], sm[:, 0:2], -SCALE, None, ALU.mult).then_inc(score_max, 1)

            def back(l, i):
                kind, h = UNITS[i]
                x = pr[i % 2]
                dve.wait_ge(exp_done, 13 * l + i + 1)
                if i >= 1:
                    dve.wait_ge(task_ps, l * N_TASK + TASK["w", i - 1] + 1)
                sm = small[:, 12 * (i % 4):12 * (i % 4) + 12]
                if kind == "meta":
                    xm = x[0:NMETA].rearrange("p m n -> p (m n)")[:, 0:128].rearrange("p (g n) -> p g n", g=8)
                    s = small[0:NMETA, 56:64]
                    then(dve.tensor_reduce(s, xm, X, ALU.add))
                    then(dve.reciprocal(small[0:NMETA, 64:72], s))
                    x2 = small[0:NMETA, 68:72]
                    then(dve.tensor_scalar(x2, x2, lam[0:NMETA, l:l + 1], None, ALU.mult))
                    then(dve.tensor_tensor(xm, xm, small[0:NMETA, 64:72].unsqueeze(2).broadcast_to([NMETA, 8, NMETA]),
                                           ALU.mult))
                    w_read[i] = did(dve.tensor_tensor(
                        Wt[0:NMETA, 0:64].rearrange("p (h n) -> p h n", h=HEADS), xm[:, 0:4, :], xm[:, 4:8, :],
                        ALU.add))
                else:
                    n = {"frames1": 272, "frames0": 144, "decode": 256}[kind]
                    then(dve.reciprocal(sm[:, 6:8], sm[:, 4:6]))
                    c = did(dve.tensor_scalar(sm[:, 8:9], sm[:, 7:8], lam[:, l:l + 1], None, ALU.mult))
                    c = did(dve.tensor_scalar(Wt[:, 0:n], x[:, 0, 0:n], sm[:, 6:7], None, ALU.mult))
                    after(c)
                    w_read[i] = did(dve.scalar_tensor_tensor(Wt[:, 0:n], x[:, 1, 0:n], sm[:, 8:9], Wt[:, 0:n],
                                                             ALU.mult, ALU.add))
                after(w_read[i])
                dve.sem_inc(w_done, 1)

            def task(l, kind, n):
                i = TASK[kind, n]
                bank = 4 + i % 2
                dve.wait_ge(task_ps, l * N_TASK + i + 1)
                if kind == "cachek":
                    dve.tensor_copy(kct.rearrange("p h k -> p (h k)"), PS[:, bank, :]).then_inc(task_dve, 1)
                elif kind == "past":
                    dve.tensor_copy(ST[:, :, :, n * DS:(n + 1) * DS],
                                    PS[:, bank, 0:128].rearrange("p (h m t) -> p h m t", h=HEADS, m=2)
                                    ).then_inc(task_dve, 1)
                else:
                    what, h = UNITS[n]
                    wt = WT[n % 2]
                    if what in ("frames1", "frames0"):
                        nb = 2 if what == "frames1" else 1
                        dve.tensor_copy(wt[:, 0:nb, :], PS[:, bank, 0:nb * P].rearrange("p (k q) -> p k q", k=nb))
                        dve.tensor_copy(wt[0:NMETA, nb, :], PS[0:NMETA, bank, nb * P:(nb + 1) * P]
                                        ).then_inc(task_dve, 1)
                    elif what == "decode":
                        dve.tensor_copy(WTp[:, h, :], PS[:, bank, 0:P])
                        dve.tensor_copy(wt[:, 1, :], PS[:, bank, P:2 * P]).then_inc(task_dve, 1)
                    else:
                        dve.tensor_copy(wt[0:NMETA, 0, 0:64], PS[0:NMETA, bank, 0:64]).then_inc(task_dve, 1)

            def route(l):
                lg, pb, sel, t0, t1, oh1, oh2, rk = RT[0:8]
                mask = RT[13]

                def tt(out, a, b, op):
                    then(dve.tensor_tensor(out, a, b, op))

                def ts(out, a, s1, s2, o1, o2=None):
                    then(dve.tensor_scalar(out, a, s1, s2, o1, o2) if o2 is not None
                         else dve.tensor_scalar(out, a, s1, s2, o1))

                def red(out, a, op):
                    then(dve.tensor_reduce(out, a, X, op))

                def wide(a, n=NE):
                    return a.unsqueeze(2).broadcast_to([P, 4, n])

                pri = CT[:, C_PE:C_PE + NE].unsqueeze(1).broadcast_to([P, 4, NE])
                prig = CT[:, C_PG:C_PG + NG].unsqueeze(1).broadcast_to([P, 4, NG])
                valid = CT[:, C_VALID:C_VALID + 4] if l + 1 < DEPTH else CT[:, C_LAST:C_LAST + 4]
                dve.wait_ge(lg_ps, 2 * (l + 1))
                dve.tensor_copy(lgT, PS[0:NE, 0, 0:NTOK]).then_inc(lg_sb, 1)
                then(dve.memset(lg, 0.0))
                dve.wait_ge(lgt_ps, l + 1)
                c = did(dve.tensor_copy(lg[:, 0:3, :], PS[:, 1, 0:48].rearrange("p (t e) -> p t e", t=3)))
                c = did(dve.tensor_copy(lg[0:NMETA, 3, :], PS[0:NMETA, 1, 48:64]))
                after(c)
                red(r4[0], lg, ALU.max)
                dve.tensor_tensor(lg, lg, wide(r4[0]), ALU.subtract).then_inc(lg_shifted, 1)
                dve.wait_ge(act_step, l + 1)
                red(r4[1], lg, ALU.add)
                then(dve.reciprocal(r4[2], r4[1]))
                tt(pb, lg, wide(r4[2]), ALU.mult)
                tt(sel, pb, rb_[:, :].unsqueeze(1).broadcast_to([P, 4, NE]), ALU.add)
                s4 = sel.rearrange("p t (g e) -> p t g e", g=NG)
                c = did(dve.tensor_tensor(pairs6[:, :, :, 0:3], s4[:, :, :, 0:3], s4[:, :, :, 1:4], ALU.add))
                c = did(dve.tensor_tensor(pairs6[:, :, :, 3:5], s4[:, :, :, 0:2], s4[:, :, :, 2:4], ALU.add))
                c = did(dve.tensor_tensor(pairs6[:, :, :, 5:6], s4[:, :, :, 0:1], s4[:, :, :, 3:4], ALU.add))
                after(c)
                red(g4[0], pairs6, ALU.max)
                red(r4[3], g4[0], ALU.max)
                tt(g4[1], g4[0], wide(r4[3], NG), ALU.is_ge)
                tt(g4[2], g4[1], prig, ALU.mult)
                red(r4[4], g4[2], ALU.max)
                tt(g4[3], g4[2], wide(r4[4], NG), ALU.is_equal)
                gw = g4[3].unsqueeze(3).broadcast_to([P, 4, NG, EPG])
                then(dve.tensor_tensor(t0.rearrange("p t (g e) -> p t g e", g=NG), s4, gw, ALU.mult))
                ts(g4[2], g4[3], 1.0, -NEG, ALU.subtract, ALU.mult)
                gw = g4[2].unsqueeze(3).broadcast_to([P, 4, NG, EPG])
                t04 = t0.rearrange("p t (g e) -> p t g e", g=NG)
                then(dve.tensor_tensor(t04, t04, gw, ALU.add))
                for n, oh in ((0, oh1), (1, oh2)):
                    red(r4[5], t0, ALU.max)
                    tt(t1, t0, wide(r4[5]), ALU.is_ge)
                    tt(t1, t1, pri, ALU.mult)
                    red(r4[6], t1, ALU.max)
                    tt(oh, t1, wide(r4[6]), ALU.is_equal)
                    tt(t1, oh, pb, ALU.mult)
                    red(gates[:, n, :], t1, ALU.add)
                    if n == 0:
                        ts(t1, oh, NEG, None, ALU.mult)
                        tt(t0, t0, t1, ALU.add)
                    tt(oh, oh, wide(valid), ALU.mult)
                tt(mask, oh1, oh2, ALU.add)
                dve.sem_inc(hot_done, 1)
                tt(r4[7], gates[:, 0, :], gates[:, 1, :], ALU.add)
                then(dve.reciprocal(r4[8], r4[7]))
                tt(gates[:, 0, :], gates[:, 0, :], r4[8], ALU.mult)
                tt(gates[:, 1, :], gates[:, 1, :], r4[8], ALU.mult)
                for k, oh in ((0, oh1), (1, oh2)):
                    tt(vals[:, k, :, 0:NE], oh, wide(CT[:, C_ROW:C_ROW + 4]), ALU.mult)
                    tt(vals[:, k, :, NE:2 * NE], oh, wide(CT[:, C_ROW + 4 * k:C_ROW + 4 * k + 4]), ALU.mult)
                dve.wait_ge(rank_ps, l + 1)
                then(dve.tensor_copy(rk, PS[:, 2, 0:64].rearrange("p (t e) -> p t e", t=4)))
                tot = t0
                then(dve.tensor_copy(tot, PS[:, 3, 0:64].rearrange("p (t e) -> p t e", t=4)))
                for j in range(1, 4):
                    tt(rk[:, j:4, :], rk[:, j:4, :], tot[:, j - 1:j, :].broadcast_to([P, 4 - j, NE]), ALU.add)
                tt(t1[:, 0, :], tot[:, 0, :], tot[:, 1, :], ALU.add)
                tt(t1[:, 1, :], tot[:, 2, :], tot[:, 3, :], ALU.add)
                tt(t1[:, 2, :], t1[:, 0, :], t1[:, 1, :], ALU.add)
                red(r4[9][:, 0:1], t1[:, 2, :], ALU.max)
                ts(r4[9][:, 1:2], r4[9][:, 0:1], float(P), None, ALU.is_gt)
                ts(r4[9][:, 2:3], r4[9][:, 0:1], float(2 * P), None, ALU.is_gt)
                ts(r4[9][:, 3:4], r4[9][:, 0:1], float(3 * P), None, ALU.is_gt)
                red(r4[10][:, 0:1], r4[9][:, 1:4], ALU.add)
                dve.tensor_copy(more_rounds[:, :], r4[10][0:1, 0:1]).then_inc(routed, 1)
                for k, oh in ((0, oh1), (1, oh2)):
                    tt(t1, oh, rk, ALU.mult)
                    red(r4[k], t1, ALU.add)

            def moe_round(l, rb, r):
                for k in range(2):
                    last = dve.tensor_tensor(hot[k], CT[:, C_IOTA:C_IOTA + P].unsqueeze(1).broadcast_to([P, 4, P]),
                                             r4[k].unsqueeze(2).broadcast_to([P, 4, P]), ALU.is_equal)
                last.then_inc(idx_in, 1)
                dve.wait_ge(idx_ps, rb + r + 1)
                dve.tensor_scalar(idx[:, :, :], PS[:, 7, 0:2 * NE].rearrange("p (k e) -> p k e", k=2), FAR, None,
                                  ALU.add).then_inc(idx_ready, 1)

                def turned(i, par):
                    E = 16 * (rb + r) + 2 * i + par
                    dve.wait_ge(xt_hi, E + 1)
                    dve.tensor_tensor(x_lo[par][:, :].rearrange("p (b n) -> p b n", b=2), PS[:, 2:4, :],
                                      x_hi[par][:, :].bitcast(F32).rearrange("p (b n) -> p b n", b=2), ALU.subtract
                                      ).then_inc(xt_lo, 1)

                def split_up(i, par, n, js):
                    E = 16 * (rb + r) + 2 * i + par
                    for j in js:
                        w, lo = quarter(3 * par + n, j)
                        dve.wait_ge(up_hi, 8 * E + 4 * n + j + 1)
                        dve.tensor_tensor(lo, w, w_hi[j][:, :].bitcast(F32), ALU.subtract).then_inc(up_lo, 1)

                def split_down(i, par, js):
                    E = 16 * (rb + r) + 2 * i + par
                    for j in js:
                        w, lo = quarter(5 if par == 0 else 2, j)
                        dve.wait_ge(down_hi, 4 * E + j + 1)
                        dve.tensor_tensor(lo, w, w_hi[j][:, :].bitcast(F32), ALU.subtract
                                          ).then_inc(down_lo, 1)

                def gated(i, par):
                    E = 16 * (rb + r) + 2 * i + par
                    dve.wait_ge(silu_done, E + 1)
                    dve.wait_ge(up_used, 8 * E + 8)
                    dve.tensor_tensor(hid, hid, PS[:, 1, :], ALU.mult).then_inc(hid_done, 1)

                def hid_turned(i, par):
                    E = 16 * (rb + r) + 2 * i + par
                    dve.wait_ge(ht_hi, E + 1)
                    dve.tensor_tensor(h_lo[:, :], PS[:, 4, :], h_hi[:, :].bitcast(F32), ALU.subtract).then_inc(ht_lo, 1)

                def pair(i, first, last):
                    split_up(i, 0, 0, range(3))
                    if not first:
                        hid_turned(i - 1, 1)
                    split_up(i, 0, 0, range(3, 4))
                    split_up(i, 0, 1, range(4))
                    if not first:
                        split_down(i - 1, 1, range(3))
                    gated(i, 0)
                    if not first:
                        split_down(i - 1, 1, range(3, 4))
                    turned(i, 1)
                    split_up(i, 1, 0, range(3))
                    hid_turned(i, 0)
                    split_up(i, 1, 0, range(3, 4))
                    split_up(i, 1, 1, range(4))
                    split_down(i, 0, range(3))
                    gated(i, 1)
                    split_down(i, 0, range(3, 4))
                    if not last:
                        turned(i + 1, 0)

                turned(0, 0)
                pair(0, True, False)
                with dve.Fori(1, PAIRS - 1) as i:
                    pair(i, False, False)
                pair(PAIRS - 1, False, True)
                hid_turned(PAIRS - 1, 1)
                split_down(PAIRS - 1, 1, range(4))
                dve.wait_ge(round_closed, rb + r + 1)
                for k in range(2):
                    last = dve.tensor_scalar(r4[k], r4[k], float(P), None, ALU.subtract)
                    last.then_inc(rank_moved, 1)
                dve.wait_ge(rank_moved, 2 * (rb + r) + 2)

            w_read = {}
            then(dve.memset(lam[:, 6:7], EPS))
            then(dve.memset(qz[:, :, :, :, :].rearrange("p h b m t -> p (h b m t)"), 0.0))
            dve.wait_ge(x_in, 64)
            for j in range(4):
                ln_front(0, j)
            for j in range(4):
                ln_back(0, j)
            dve.wait_ge(cols_in, 16 * (2 + 8 + 1))
            l4 = lq.rearrange("p l (i d) -> p l i d", i=4)
            for l in range(DEPTH):
                then(dve.tensor_tensor(l4[:, l, 0:4:2, :], l4[:, l, 0:4:2, :], l4[:, l, 1:4:2, :], ALU.mult))
                last = dve.tensor_reduce(lam[:, 2 + 2 * l:4 + 2 * l], l4[:, l, 0:4:2, :], X, ALU.add)
                last.then_inc(lam_sum, 1)
            dve.wait_ge(lam_exp, 1)
            for l in range(DEPTH):
                then(dve.tensor_tensor(lam[:, l:l + 1], lam[:, 3 + 2 * l:4 + 2 * l], lam[:, 2 + 2 * l:3 + 2 * l],
                                       ALU.subtract))
                then(dve.tensor_scalar(lam[:, l:l + 1], lam[:, l:l + 1], -LAM_INIT[l], None, ALU.add))
                then(dve.tensor_scalar(cols[:, l:l + 1], cols[:, l:l + 1], 1.0 - LAM_INIT[l], None, ALU.mult))
            dve.sem_inc(lam_done, 1)
            turn_h(0)
            rb = 0
            for l in range(DEPTH):
                dve.wait_ge(proj_sb, 16 * l + 4)
                for m in range(2):
                    last = dve.tensor_copy(qz[64 * m:64 * m + 64, :, :, m, :],
                                           qT[64 * m:64 * m + 64, :, DEC:NTOK].rearrange("p h (b t) -> p h b t", b=DB))
                last.then_inc(qz_done, 1)
                for j in range(STEPS):
                    if j < 8:
                        task(l, "cachek", j)
                        task(l, "past", j)
                    if j < len(UNITS):
                        front(l, j)
                    if j >= 2:
                        task(l, "w", j - 2)
                    if 1 <= j <= len(UNITS):
                        back(l, j - 1)
                for h in range(HEADS):
                    rs = pr[h % 2].rearrange("p m n -> p (m n)")[:, 0:NTOK]
                    dve.wait_ge(rms_done, 4 * l + h + 1)
                    then(dve.reciprocal(rs, rs))
                    dve.scalar_tensor_tensor(FT[:, h, :], OT[:, h, :], cols[:, l:l + 1], rs, ALU.mult,
                                             ALU.mult).then_inc(mix_done, 1)
                q = LN1[l]
                for j in tiles_of(l):
                    n = TN[j]
                    dve.wait_ge(op_ps, 4 * l + j + 1)
                    b = 6 * (j % 2)
                    c = did(dve.scalar_tensor_tensor(H[0:n, j, :], H[0:n, j, :], ALPHA,
                                                     PS[0:n, b:b + 2, :].rearrange("p k n -> p (k n)"), ALU.mult,
                                                     ALU.add))
                    after(c)
                    dve.sem_inc(res_done, 1)
                    ln_front(q, j)
                    ln_back(q, j)
                turn_h(q)
                route(l)
                more = dve.value_load(more_rounds[0:1, 0:1], min_val=0, max_val=3)
                R = more + 1
                with dve.Fori(0, R) as r:
                    moe_round(l, rb, r)
                rb = rb + R
                q = LN2[l]
                tiles = tiles_of(l)
                for j in tiles:
                    n = TN[j]
                    y = yb[j][0:n]
                    dve.wait_ge(y_scaled, 4 * l + j + 1)
                    then(dve.scalar_tensor_tensor(y[:, 0, :], y[:, 1, :], gates[0:n, 1, j:j + 1], y[:, 0, :], ALU.mult,
                                                  ALU.add))
                    c = did(dve.scalar_tensor_tensor(H[0:n, j, :], H[0:n, j, :], ALPHA, y[:, 0, :], ALU.mult, ALU.add))
                    after(c)
                    dve.sem_inc(comb, 1)
                    ln_front(q, j)
                    if j >= 1:
                        ln_back(q, j - 1)
                ln_back(q, tiles[-1])
                if l + 1 < DEPTH:
                    turn_h(q)

        @block.scalar
        def _(act):
            def load_gb(q, g, b):
                for k, row in ((0, g), (1, b)):
                    act.dma_start(gb[:, k, :], row.partition_broadcast(P)).then_inc(gb_in, 16)

            def load_ckv(l, n):
                if n >= 8:
                    if n < 12:
                        act.wait_ge(task_ps, l * N_TASK + TASK["cachek", n - 4] + 1)
                    else:
                        act.wait_ge(cv_used, 8 * l + n - 11)
                elif n >= 4:
                    act.wait_ge(task_ps, l * N_TASK + TASK["cachek", n - 4] + 1)
                src = t["cache_k"] if n < 8 else t["cache_v"]
                act.dma_start(ckv[n % 4], src[l, n % 8].rearrange("s h e -> s (h e)")).then_inc(ckv_in[n % 4], 16)

            def turn_h(q):
                for j in ln_tiles(q):
                    bank = 3 + 2 * (j % 2)
                    act.wait_ge(hx_ps, 8 * q + 2 * j + 2)
                    act.activation(FT[:, 4:8, TC[j]:TC[j] + TN[j]],
                                   PS[:, bank, :].rearrange("p (k n) -> p k n", k=4)[:, :, 0:TN[j]],
                                   ACT.Copy).then_inc(hx_act, 1)

            def scale_y(l, j):
                y = yb[j][0:TN[j], 0, :]
                act.wait_ge(y_in[j], 16 * (l + 1))
                act.activation(y, y, ACT.Copy, scale=gates[0:TN[j], 0, j:j + 1]).then_inc(y_scaled, 1)

            def proj(l, m):
                act.wait_ge(proj_ps, 16 * l + m + 1)
                if m < 4:
                    dst = qT[:, m, :]
                elif m < 8:
                    dst = kT[:, m - 4, :]
                elif m < 12:
                    dst = vT
                    if m > 8:
                        act.wait_ge(task_ps, l * N_TASK + TASK["vu", m - 9] + 1)
                else:
                    dst = D4[:, m - 12, :]
                act.activation(dst, PS[:, m % 2, 0:NTOK], ACT.Copy).then_inc(proj_sb, 1)

            def task(l, kind, n):
                i = TASK[kind, n]
                bank = 4 + i % 2
                act.wait_ge(task_ps, l * N_TASK + i + 1)
                done = emptied(l, i)[1]
                if kind == "state":
                    act.activation(stT, PS[:, bank, 0:480].rearrange("p (g n) -> p g n", g=4),
                                   ACT.Copy).then_inc(task_act, 1)
                elif kind == "k" or n < 4:
                    dst = kout if kind == "k" else V[:, :, n * P:(n + 1) * P]
                    if kind == "k" and (n > 0):
                        act.wait_ge(k_out, 48 * (4 * l + n))
                    act.activation(dst[:, 0:3, :], PS[:, bank, 0:384].rearrange("p (t e) -> p t e", t=3), ACT.Copy)
                    act.activation(dst[0:NMETA, 3, :], PS[0:NMETA, bank, 384:512], ACT.Copy).then_inc(task_act, 1)
                    if kind == "k":
                        act.wait_ge(task_act, done)
                        act.dma_start(o["new_k_prompt"][l, 0, NMETA:, n, :].rearrange("(t p) e -> p t e", p=P),
                                      kout[:, 0:2, :]).then_inc(k_out, 16)
                        act.dma_start(o["new_k_sample"][l, :, :, n, :].rearrange("b t e -> (b t) e"),
                                      kout[:, 2, :]).then_inc(k_out, 16)
                        act.dma_start(o["new_k_prompt"][l, 0, 0:NMETA, n, :], kout[0:NMETA, 3, :]).then_inc(k_out, 16)
                    elif n == 3:
                        act.wait_ge(task_act, done)
                        act.dma_start(o["new_v_prompt"][l, 0, NMETA:].rearrange("(t p) h e -> p t (h e)", p=P),
                                      V[:, 0:2, :]).then_inc(v_out, 16)
                        act.dma_start(o["new_v_sample"][l].rearrange("b t h e -> (b t) (h e)"),
                                      V[:, 2, :]).then_inc(v_out, 16)
                        act.dma_start(o["new_v_prompt"][l, 0, 0:NMETA].rearrange("t h e -> t (h e)"),
                                      V[0:NMETA, 3, :]).then_inc(v_out, 16)
                else:
                    g = n - 4
                    if g > 0:
                        act.wait_ge(u_out, 32 * (4 * l + g))
                    act.activation(uout, PS[:, bank, 0:256].rearrange("p (t e) -> p t e", t=2),
                                   ACT.Copy).then_inc(task_act, 1)
                    act.wait_ge(task_act, done)
                    act.dma_start(o["new_pool_prompt"][l, 0, :, g * P:(g + 1) * P],
                                  uout[P - STATE:P, 0, :]).then_inc(u_out, 16)
                    act.dma_start(us[l, :, :, g * P:(g + 1) * P].rearrange("b t e -> (b t) e"),
                                  uout[:, 1, :]).then_inc(u_out, 16)

            def exps(l, i):
                kind, h = UNITS[i]
                x = pr[i % 2]
                act.wait_ge(score_max, 13 * l + i + 1)
                if kind == "meta":
                    xm = x[0:NMETA].rearrange("p m n -> p (m n)")[:, 0:128]
                    act.activation(xm, xm, ACT.Exp, scale=SCALE).then_inc(exp_done, 1)
                    return
                n = {"frames1": 272, "frames0": 144, "decode": 256}[kind]
                sm = small[:, 12 * (i % 4):12 * (i % 4) + 12]
                for m in range(2):
                    last = act.activation(x[:, m, 0:n], x[:, m, 0:n], ACT.Exp, bias=sm[:, 2 + m:3 + m], scale=SCALE,
                                          accum_out=sm[:, 4 + m:5 + m])
                last.then_inc(exp_done, 1)

            def heads_out(l, i):
                kind, h = UNITS[i]
                n = i if i < 8 else 8
                if kind == "decode":
                    return
                act.wait_ge(av_ps, 9 * l + n + 1)
                if kind == "meta":
                    act.activation(OT[:, :, 0:NMETA], PS[:, 1, 0:64].rearrange("p (h q) -> p h q", h=HEADS),
                                   ACT.Copy).then_inc(ot_sb, 1)
                else:
                    c = TC[1] if kind == "frames1" else TC[0]
                    act.activation(OT[:, h, c:c + P], PS[:, 6 + i % 2, 0:P], ACT.Copy).then_inc(ot_sb, 1)

            def moe_round(l, rb, r):
                base = round_use(l, rb, r)
                E0 = 16 * (rb + r)

                def turned(i, par):
                    E = E0 + 2 * i + par
                    act.wait_ge(xt_ps, E + 1)
                    act.activation(x_hi[par][:, :].rearrange("p (b n) -> p b n", b=2), PS[:, 2:4, :], ACT.Copy
                                   ).then_inc(xt_hi, 1)

                def split_up(i, par, n, js):
                    E = E0 + 2 * i + par
                    for j in js:
                        if j == 0:
                            act.wait_ge(landed[3 * par + n], 16 * (base + i + 1))
                        if n == 1:
                            act.wait_ge(up_used, 8 * E + j + 1)
                        elif not (isinstance(i, int) and i == 0):
                            act.wait_ge(down_used, 4 * E - 8 + j + 1)
                        elif par == 1:
                            act.wait_ge(up_used, 8 * E0 + 4 + j + 1)
                        act.activation(w_hi[j][:, :], quarter(3 * par + n, j)[0], ACT.Copy).then_inc(up_hi, 1)

                def split_down(i, par, js, last=False):
                    E = E0 + 2 * i + par
                    for j in js:
                        if j == 0:
                            act.wait_ge(landed[5 if par == 0 else 2], 16 * (base + i + 1))
                        if last:
                            act.wait_ge(down_used, 4 * E - 4 + j + 1)
                        else:
                            act.wait_ge(up_used, 8 * E + 12 + j + 1)
                        act.activation(w_hi[j][:, :], quarter(5 if par == 0 else 2, j)[0], ACT.Copy).then_inc(down_hi, 1)

                def silu(i, par):
                    E = E0 + 2 * i + par
                    act.wait_ge(up_used, 8 * E + 4)
                    act.activation(hid, PS[:, 0, :], ACT.Silu).then_inc(silu_done, 1)

                def hid_turned(i, par):
                    E = E0 + 2 * i + par
                    act.wait_ge(ht_ps, E + 1)
                    act.activation(h_hi[:, :], PS[:, 4, :], ACT.Copy).then_inc(ht_hi, 1)

                def result(i, par):
                    E = E0 + 2 * i + par
                    act.wait_ge(down_used, 4 * E + 4)
                    if not (isinstance(i, int) and i == 0):
                        act.wait_ge(scat[par], 16 * (PAIRS * (rb + r) + i))
                    act.activation(ob[par].rearrange("p (b n) -> p b n", b=2), PS[:, 5:7, :], ACT.Copy
                                   ).then_inc(o_sb, 1)

                def pair(i, first, last):
                    split_up(i, 0, 0, range(3))
                    if not first:
                        hid_turned(i - 1, 1)
                        result(i - 1, 0)
                    split_up(i, 0, 0, range(3, 4))
                    split_up(i, 0, 1, range(4))
                    silu(i, 0)
                    if not first:
                        split_down(i - 1, 1, range(4))
                    turned(i, 1)
                    split_up(i, 1, 0, range(3))
                    hid_turned(i, 0)
                    if not first:
                        result(i - 1, 1)
                    split_up(i, 1, 0, range(3, 4))
                    split_up(i, 1, 1, range(4))
                    silu(i, 1)
                    split_down(i, 0, range(4))
                    if not last:
                        turned(i + 1, 0)

                turned(0, 0)
                pair(0, True, False)
                pair(1, False, False)
                with act.Fori(2, PAIRS - 1) as i:
                    pair(i, False, False)
                pair(PAIRS - 1, False, True)
                hid_turned(PAIRS - 1, 1)
                result(PAIRS - 1, 0)
                split_down(PAIRS - 1, 1, range(4), last=True)
                result(PAIRS - 1, 1)

            act.dma_start(H[:, 0:2, :], t["x_prompt"][0].rearrange("(t p) n -> p t n", p=P)).then_inc(x_in, 16)
            act.dma_start(H[:, 2, :], t["x_sample"].rearrange("b t n -> (b t) n")).then_inc(x_in, 16)
            act.dma_start(H[0:NMETA, 3, :], t["meta_tokens"]).then_inc(x_in, 16)
            act.dma_start(rb_[:, :], t["router_b"].partition_broadcast(P)).then_inc(x_in, 16)
            load_gb(0, t["ln_in_g"], t["ln_in_b"])
            act.dma_start(CT[:, :], t["consts"]).then_inc(consts_in, 16)
            for l in range(DEPTH):
                act.dma_start(cols[:, l:l + 1], t["subln_w"][l].rearrange("(p o) -> p o", o=1)).then_inc(cols_in, 16)
                for g in range(4):
                    act.dma_start(cols[:, 2 + 4 * l + g:3 + 4 * l + g],
                                  t["pool_scale"][l, g * P:(g + 1) * P].rearrange("(p o) -> p o", o=1)
                                  ).then_inc(cols_in, 16)
            act.dma_start(lq.rearrange("p l n -> p (l n)"),
                          t["lambda_qk"].rearrange("l i d -> (l i d)").partition_broadcast(P)).then_inc(cols_in, 16)
            act.dma_start(rw[:, :, :], t["router_w"].rearrange("(k p) e -> p k e", p=P)).then_inc(consts_in, 16)
            act.wait_ge(lam_sum, DEPTH)
            act.activation(lam[:, 2:6], lam[:, 2:6], ACT.Exp).then_inc(lam_exp, 1)
            turn_h(0)
            rb = 0
            for l in range(DEPTH):
                if l == 0:
                    act.wait_ge(lam_done, 1)
                act.dma_start(spin[0:120, :], t["state_pool"][l].rearrange("b s n -> (b s) n")).then_inc(state_in, 16)
                for n in range(4):
                    load_ckv(l, n)
                act.dma_start(wpool[:, :, :], t["w_pool"][l].rearrange("g c e -> c g e")).then_inc(wpool_in, 16)
                for m in range(8):
                    proj(l, m)
                task(l, "state", 0)
                for j in range(STEPS):
                    if j < 8:
                        load_ckv(l, 4 + j)
                    if j in BLOCK_AT:
                        proj(l, 8 + BLOCK_AT[j])
                    if j < 4:
                        task(l, "k", j)
                    if j - 1 in BLOCK_AT:
                        task(l, "vu", BLOCK_AT[j - 1])
                    if j < len(UNITS):
                        exps(l, j)
                    if j >= 2:
                        heads_out(l, j - 2)
                for n in range(12, 16):
                    load_ckv(l, n)
                for g in range(4):
                    act.wait_ge(pm_ps, 4 * l + g + 1)
                    act.activation(FT[:, 4 + g, :], PS[:, 6 + g % 2, 0:NTOK], ACT.Copy,
                                   scale=cols[:, 2 + 4 * l + g:3 + 4 * l + g]).then_inc(pm_sb, 1)
                act.wait_ge(cv_used, 8 * (l + 1))
                act.activation(OT[:, :, DEC:NTOK], PS[:, 0, :].rearrange("p (h q) -> p h q", h=HEADS),
                               ACT.Copy).then_inc(ot_sb, 1)
                act.wait_ge(ot_sb, 10 * (l + 1))
                for h in range(HEADS):
                    act.activation(FT[:, h, :], OT[:, h, :], ACT.Square).then_inc(sq_done, 1)
                for h in range(HEADS):
                    act.wait_ge(ss_ps, 4 * l + h + 1)
                    if h >= 2:
                        act.wait_ge(mix_done, 4 * l + h - 1)
                    act.activation(pr[h % 2].rearrange("p m n -> p (m n)")[:, 0:NTOK], PS[:, 2 + h, 0:NTOK], ACT.Sqrt,
                                   bias=lam[:, 6:7], scale=1.0 / P).then_inc(rms_done, 1)
                act.wait_ge(u_out, 128 * (l + 1))
                act.dma_start(o["new_pool_sample"][l], us[l, :, 1:DS, :]).then_inc(us_out, 16)
                act.wait_ge(mix_done, 4 * (l + 1))
                act.wait_ge(v_out, 48 * (l + 1))
                load_gb(LN1[l], t["ln1_g"][l], t["ln1_b"][l])
                turn_h(LN1[l])
                act.wait_ge(lg_shifted, l + 1)
                act.activation(RT[0].rearrange("p t e -> p (t e)"), RT[0].rearrange("p t e -> p (t e)"),
                               ACT.Exp).then_inc(act_step, 1)
                act.wait_ge(routed, l + 1)
                more = act.value_load(more_rounds[0:1, 0:1], min_val=0, max_val=3)
                R = more + 1
                with act.Fori(0, R) as r:
                    moe_round(l, rb, r)
                rb = rb + R
                act.wait_ge(round_closed, rb)
                tiles = tiles_of(l)
                for j in tiles:
                    act.dma_start(yb[j][0:TN[j]],
                                  ys.rearrange("(k r) n -> k r n", k=2)[:, P * j:P * j + TN[j], :]
                                  .rearrange("k r n -> r k n")).then_inc(y_in[j], 16)
                    if j == 0:
                        load_gb(LN2[l], t["ln2_g"][l], t["ln2_b"][l])
                for j in tiles:
                    scale_y(l, j)
                if l + 1 < DEPTH:
                    turn_h(LN2[l])
                    act.wait_ge(comb, 4 * (l + 1))
            act.wait_ge(k_out, 48 * 4 * DEPTH)
            act.wait_ge(v_out, 48 * DEPTH)
            act.wait_ge(u_out, 128 * DEPTH)
            act.wait_ge(us_out, 16 * DEPTH)

        @block.gpsimd
        def _(pool):
            steps = [0]

            def then(ins):
                steps[0] += 1
                ins.then_inc(pool_step, 1)
                pool.wait_ge(pool_step, steps[0])

            half = CT[:, C_HALF:C_HALF + 1]

            def ln_power(q, j):
                n = TN[j]
                pool.wait_ge(ln_var, ln_count(q, j))
                pool.tensor_tensor(stats[0:n, j, 15:16], stats[0:n, j, 14:15], half[0:n, 0:1], ALU.pow
                                   ).then_inc(ln_rstd, 1)

            def ln_bias(q, j):
                n = TN[j]
                pool.wait_ge(ln_scaled, ln_count(q, j))
                pool.tensor_tensor(H[0:n, j, :], H[0:n, j, :], gb[0:n, 1, :], ALU.add).then_inc(ln_out, 1)

            def pooling(l, g):
                w = WINDOWS[g]
                pool.wait_ge(proj_sb, 16 * l + 13 + g)
                dec = ue[:, EXT:EW].rearrange("p (b n) -> p b n", b=DB)
                if 4 * l + g > 0:
                    pool.wait_ge(d4_done, 4 * l + g)
                pool.memset(ue[:, 0:STATE], 0.0)
                pool.tensor_copy(ue[:, STATE:EXT], D4[:, g, 0:NMETA + SEQ])
                if g == 0:
                    pool.wait_ge(task_act, emptied(l, TASK["state", 0])[1])
                pool.tensor_copy(dec[:, :, 0:STATE], stT[:, g, :].rearrange("p (b n) -> p b n", b=DB))
                then(pool.tensor_copy(dec[:, :, STATE:STATE + DS],
                                      D4[:, g, DEC:NTOK].rearrange("p (b n) -> p b n", b=DB)))
                src, s, lo = ue, 1, 0
                for n in range(g + 1):
                    dst = (wa, wb)[n % 2]
                    lo += s
                    then(pool.tensor_tensor(dst[:, lo:EW], src[:, lo:EW], src[:, lo - s:EW - s], ALU.add))
                    src, s = dst, 2 * s
                win = src
                then(pool.tensor_tensor(win[:, STATE:STATE + NMETA], win[:, STATE:STATE + NMETA],
                                        CT[:, C_POOL + NMETA * g:C_POOL + NMETA * (g + 1)], ALU.mult))
                then(pool.tensor_scalar(win[:, STATE:EW], win[:, STATE:EW], 1.0 / w, 0.0, ALU.mult, ALU.add))
                pool.wait_ge(task_ps, l * N_TASK + TASK["vu", 4 + g] + 1)
                then(pool.tensor_tensor(D4[:, g, 0:NMETA + SEQ], win[:, STATE:EXT], ue[:, STATE:EXT], ALU.subtract))
                pool.tensor_tensor(D4[:, g, DEC:NTOK].rearrange("p (b n) -> p b n", b=DB),
                                   win[:, EXT:EW].rearrange("p (b n) -> p b n", b=DB)[:, :, STATE:STATE + DS],
                                   dec[:, :, STATE:STATE + DS], ALU.subtract).then_inc(d4_done, 1)

            last_row, last_result = pool.to_reg(NTOK - 1), pool.to_reg(2 * NTOK - 1)

            def gather(e):
                pool.indirect_dma_start(xg[e % 2], None, xs, bass.IndirectOffsetOnAxis(ap=idx[:, 0, e:e + 1], axis=0),
                                        bounds_check=last_row, oob_is_err=False).then_inc(xg_in[e % 2], 16)

            def moe_round(l, rb, r):
                E0 = 16 * (rb + r)
                pool.wait_ge(idx_ready, rb + r + 1)
                pool.sem_inc(pool_past_wait, 1)
                gather(0)
                gather(1)
                for e in range(NE):
                    if e + 2 < NE:
                        pool.wait_ge(xt_ps, E0 + e + 1)
                        pool.sem_inc(pool_past_wait, 1)
                        gather(e + 2)
                    pool.wait_ge(o_sb, E0 + e + 1)
                    pool.sem_inc(pool_past_wait, 1)
                    pool.indirect_dma_start(ys, bass.IndirectOffsetOnAxis(ap=idx[:, 1, e:e + 1], axis=0), ob[e % 2],
                                            None, bounds_check=last_result, oob_is_err=False
                                            ).then_inc(scat[e % 2], 16)
                for par in range(2):
                    pool.wait_ge(scat[par], 16 * PAIRS * (rb + r + 1))
                pool.sem_inc(round_closed, 1)

            pool.wait_ge(consts_in, 32)
            for j in range(4):
                ln_power(0, j)
            pool.wait_ge(gb_in, 32)
            for j in range(4):
                ln_bias(0, j)
            rb = 0
            for l in range(DEPTH):
                for g in range(4):
                    pooling(l, g)
                for j in tiles_of(l):
                    ln_power(LN1[l], j)
                    ln_bias(LN1[l], j)
                    pool.wait_ge(ln_out, ln_count(LN1[l], j))
                    if j == tiles_of(l)[-1]:
                        pool.memset(M[:, 0:2048], 0.0).then_inc(xg_zero, 1)
                    pool.dma_start(xs[P * j:P * j + TN[j], :], H[0:TN[j], j, :]).then_inc(xs_out, 16)
                pool.wait_ge(xg_zero, l + 1)
                pool.wait_ge(xs_out, 64 * l + 16 * len(tiles_of(l)))
                pool.wait_ge(routed, l + 1)
                more = pool.value_load(more_rounds[0:1, 0:1], min_val=0, max_val=3)
                R = more + 1
                with pool.Fori(0, R) as r:
                    moe_round(l, rb, r)
                rb = rb + R
                q = LN2[l]
                tiles = tiles_of(l)
                ln_power(q, 0)
                for j in tiles:
                    if j + 1 in tiles:
                        ln_power(q, j + 1)
                    ln_bias(q, j)
                    if l + 1 == DEPTH:
                        dst = o["y_prompt"][0, P * j:P * (j + 1), :] if j < 2 else o["y_sample"].rearrange(
                            "b t n -> (b t) n")
                        pool.wait_ge(ln_out, ln_count(q, j))
                        pool.dma_start(dst, H[:, j, :]).then_inc(y_out, 16)
            pool.wait_ge(y_out, 48)


_INS = ["x_prompt", "x_sample", "cache_k", "cache_v", "state_pool", "meta_tokens", "ln_in_g", "ln_in_b", "w_in",
        "lambda_qk", "subln_w", "w_pool", "pool_scale", "w_out", "ln1_g", "ln1_b", "router_w", "router_b", "w_gate",
        "w_up", "w_down", "ln2_g", "ln2_b"]
_OUTS = [("y_prompt", (1, SEQ, D)), ("y_sample", (DB, DS, D)),
         ("new_k_prompt", (DEPTH, 1, NMETA + SEQ, HEADS, 2 * HD)), ("new_v_prompt", (DEPTH, 1, NMETA + SEQ, HEADS, 2 * HD)),
         ("new_pool_prompt", (DEPTH, 1, STATE, AW)),
         ("new_k_sample", (DEPTH, DB, DS, HEADS, 2 * HD)), ("new_v_sample", (DEPTH, DB, DS, HEADS, 2 * HD)),
         ("new_pool_sample", (DEPTH, DB, STATE, AW))]


def kernel(**inputs):
    import concourse.bacc as _bacc
    from concourse.bass_utils import run_bass_kernel_spmd as _run

    nc = _bacc.Bacc("TRN2", target_bir_lowering=False, num_devices=1)
    arrays, t, o = {}, {}, {}
    for name in _INS:
        arrays[f"in_{name}"] = np.ascontiguousarray(inputs[name])
    arrays["in_consts"] = const_table()
    for name in _INS + ["consts"]:
        a = arrays[f"in_{name}"]
        t[name] = nc.dram_tensor(f"in_{name}", a.shape, mybir.dt.from_np(a.dtype), kind="ExternalInput").ap()
    for name, shape in _OUTS:
        o[name] = nc.dram_tensor(f"out_{name}", shape, F32, kind="ExternalOutput").ap()
    program(nc, t, o)
    r = _run(nc, [arrays], core_ids=[0])
    return tuple(r.results[0][f"out_{name}"] for name, _ in _OUTS)
```
